# Optimizing a Trainium2 kernel written in Bass

```python
import math
import jax, jax.numpy as jnp
from jax import lax
import numpy as np

D_MODEL = 1024
BATCH = 1
SEQ = 1024
DEPTH = 1

MIX_WIDTH = D_MODEL
ATTN_WIDTH = MIX_WIDTH // 2
POOL_WIDTH = MIX_WIDTH - ATTN_WIDTH
N_DIFF_HEADS = 4
DIFF_HEAD_DIM = ATTN_WIDTH // N_DIFF_HEADS // 2
DIFF_V_DIM = 2 * DIFF_HEAD_DIM
POOL_WINDOWS = (2, 4, 8, 16)
N_POOL_GROUPS = len(POOL_WINDOWS)
POOL_GROUP_DIM = POOL_WIDTH // N_POOL_GROUPS
IN_WIDTH = 3 * ATTN_WIDTH + POOL_WIDTH
FF_MULTIPLE = 256
D_FF = ((8 * D_MODEL + 3 * FF_MULTIPLE - 1) // (3 * FF_MULTIPLE)) * FF_MULTIPLE
Q_BLOCK = 128
NORM_EPS = 1e-5

kernel_name = "hymba_diffattn_multiscale_pool_block"

def rms_norm(x, g):
    xf = x.astype(jnp.float32)
    y = xf * lax.rsqrt(jnp.mean(xf * xf, axis=-1, keepdims=True) + NORM_EPS)
    return (y * g.astype(jnp.float32)).astype(x.dtype)

def lambda_init(layer):
    return 0.8 - 0.6 * math.exp(-0.3 * layer)

def diff_attention(q, k, v, lam):
    seq = q.shape[1]
    scale = DIFF_HEAD_DIM ** -0.5
    q1 = jnp.transpose(q[:, :, :, 0, :], (0, 2, 1, 3)) * scale
    q2 = jnp.transpose(q[:, :, :, 1, :], (0, 2, 1, 3)) * scale
    k1 = jnp.transpose(k[:, :, :, 0, :], (0, 2, 1, 3))
    k2 = jnp.transpose(k[:, :, :, 1, :], (0, 2, 1, 3))
    vh = jnp.transpose(v, (0, 2, 1, 3)).astype(jnp.float32)
    outs = []
    for blk in range(seq // Q_BLOCK):
        start = blk * Q_BLOCK
        end = start + Q_BLOCK
        mask = jnp.arange(end)[None, :] <= (start + jnp.arange(Q_BLOCK))[:, None]
        s1 = jnp.einsum('bhqd,bhkd->bhqk', q1[:, :, start:end], k1[:, :, :end]).astype(jnp.float32)
        s2 = jnp.einsum('bhqd,bhkd->bhqk', q2[:, :, start:end], k2[:, :, :end]).astype(jnp.float32)
        s1 = jnp.where(mask, s1, -jnp.inf)
        s2 = jnp.where(mask, s2, -jnp.inf)
        attn = jax.nn.softmax(s1, axis=-1) - lam * jax.nn.softmax(s2, axis=-1)
        outs.append(jnp.einsum('bhqk,bhkv->bhqv', attn, vh[:, :, :end]))
    o = jnp.concatenate(outs, axis=2)
    return jnp.transpose(o, (0, 2, 1, 3)).astype(v.dtype)

def causal_multiscale_pool(u, pool_w, pool_scale):
    seq = u.shape[1]
    pos_count = (jnp.arange(seq) + 1)[None, :, None]
    ys = []
    for g, w in enumerate(POOL_WINDOWS):
        ug = u[..., g * POOL_GROUP_DIM:(g + 1) * POOL_GROUP_DIM].astype(jnp.float32)
        cs = jnp.cumsum(ug, axis=1)
        prev = jnp.pad(cs, ((0, 0), (w, 0), (0, 0)))[:, :seq]
        count = jnp.minimum(pos_count, w).astype(jnp.float32)
        resid = (cs - prev) / count - ug
        ys.append(jnp.einsum('bsc,cd->bsd', resid, pool_w[g].astype(jnp.float32)))
    y = jnp.concatenate(ys, axis=-1) * pool_scale.astype(jnp.float32)
    return y.astype(u.dtype)

def setup_inputs(seed: int = 0) -> dict:
    key = jax.random.key(seed)
    ks = jax.random.split(key, 14)
    f32 = jnp.float32
    def nrm(k, shape, fan_in):
        return jax.random.normal(k, shape, f32) * (fan_in ** -0.5)
    def gain(k, shape):
        return 1.0 + 0.02 * jax.random.normal(k, shape, f32)
    return {
        "x": jax.random.normal(ks[0], (BATCH, SEQ, D_MODEL), f32),
        "norm1_g": gain(ks[1], (DEPTH, D_MODEL)),
        "w_in": nrm(ks[2], (DEPTH, D_MODEL, IN_WIDTH), D_MODEL),
        "lam_qk": 0.1 * jax.random.normal(ks[3], (DEPTH, 4, DIFF_HEAD_DIM), f32),
        "subln_g": gain(ks[4], (DEPTH, DIFF_V_DIM)),
        "pool_w": nrm(ks[5], (DEPTH, N_POOL_GROUPS, POOL_GROUP_DIM, POOL_GROUP_DIM), POOL_GROUP_DIM),
        "pool_scale": gain(ks[6], (DEPTH, POOL_WIDTH)),
        "w_out": nrm(ks[7], (DEPTH, MIX_WIDTH, D_MODEL), MIX_WIDTH),
        "norm2_g": gain(ks[8], (DEPTH, D_MODEL)),
        "w_gate": nrm(ks[9], (DEPTH, D_MODEL, D_FF), D_MODEL),
        "w_up": nrm(ks[10], (DEPTH, D_MODEL, D_FF), D_MODEL),
        "w_down": nrm(ks[11], (DEPTH, D_FF, D_MODEL), D_FF),
        "final_g": gain(ks[12], (D_MODEL,)),
    }

def reference(x, norm1_g, w_in, lam_qk, subln_g, pool_w, pool_scale, w_out,
              norm2_g, w_gate, w_up, w_down, final_g):
    bsz, seq, _ = x.shape
    for layer in range(DEPTH):
        lam0 = lambda_init(layer)
        h = rms_norm(x, norm1_g[layer])
        proj = jnp.einsum('bsd,de->bse', h, w_in[layer])
        q = proj[..., :ATTN_WIDTH].reshape(bsz, seq, N_DIFF_HEADS, 2, DIFF_HEAD_DIM)
        k = proj[..., ATTN_WIDTH:2 * ATTN_WIDTH].reshape(bsz, seq, N_DIFF_HEADS, 2, DIFF_HEAD_DIM)
        v = proj[..., 2 * ATTN_WIDTH:3 * ATTN_WIDTH].reshape(bsz, seq, N_DIFF_HEADS, DIFF_V_DIM)
        u = proj[..., 3 * ATTN_WIDTH:]
        lq = lam_qk[layer].astype(jnp.float32)
        lam = (jnp.exp(jnp.sum(lq[0] * lq[1])) - jnp.exp(jnp.sum(lq[2] * lq[3])) + lam0)
        a = diff_attention(q, k, v, lam)
        a = (rms_norm(a, subln_g[layer]) * (1.0 - lam0)).reshape(bsz, seq, ATTN_WIDTH)
        p = causal_multiscale_pool(u, pool_w[layer], pool_scale[layer])
        mixed = jnp.concatenate([a, p], axis=-1)
        x = x + jnp.einsum('bse,ed->bsd', mixed, w_out[layer])
        h2 = rms_norm(x, norm2_g[layer])
        gate = jnp.einsum('bsd,df->bsf', h2, w_gate[layer])
        up = jnp.einsum('bsd,df->bsf', h2, w_up[layer])
        x = x + jnp.einsum('bsf,fd->bsd', jax.nn.silu(gate) * up, w_down[layer])
    return rms_norm(x, final_g)


_drawn_inputs = setup_inputs


def setup_inputs(seed=0):
    import zlib

    import numpy as np

    out = dict(_drawn_inputs(seed))
    spreads = {}
    factors = {'lam_qk': 8.0, 'subln_g': 5.884, 'pool_scale': 5.288, 'norm2_g': 5.004, 'final_g': 2.894}
    for name, (base, spread) in spreads.items():
        noise = np.random.default_rng([zlib.crc32(name.encode()), seed]).standard_normal(out[name].shape)
        drawn = base * np.exp(spread * noise) if base else spread * noise
        out[name] = __import__('jax').numpy.asarray(drawn.astype(out[name].dtype))
    for name, factor in factors.items():
        out[name] = (out[name] * factor).astype(out[name].dtype)
    return out
```

```python
import math
from contextlib import ExitStack

import concourse.bass as bass
from concourse import mybir

F32 = mybir.dt.float32
F32R = mybir.dt.float32r
ALU = mybir.AluOpType
ACT = mybir.ActivationFunctionType
ENG = mybir.EngineType

P = 128
BANK = 512
POOL_WINDOWS = (2, 4, 8, 16)
NORM_EPS = 1e-5
LAMBDA_INIT = 0.8 - 0.6 * math.exp(-0.3 * 0)
MASKED = -1.0e30
LOWEST = -3.0e38
DMA_SCRATCH = 1024
KIB = 1024


def hybrid_block(nc, x, norm1_g, w_in, lam_qk, subln_g, pool_w, pool_scale, w_out,
                 norm2_g, w_gate, w_up, w_down, final_g, out):
    _, SEQ, D = x.shape
    HD = lam_qk.shape[2]
    VD = subln_g.shape[1]
    POOL = pool_scale.shape[1]
    G = POOL // P
    ATTN = D - POOL
    H = ATTN // VD
    FF = w_gate.shape[2]
    NT = SEQ // P
    KD = D // P
    NF = FF // P
    STEPS = NF // 2
    HALF = SEQ // 2
    assert VD == P == 2 * HD and HALF == BANK and D == 2 * BANK and NT == KD == 8 and H == G == 4
    assert NF % 2 == 0 and STEPS % 2 == 1
    SCALE = HD ** -0.5

    with ExitStack() as ctx:
        def sem(name):
            return ctx.enter_context(nc.semaphore(name))

        R0 = 2 * KIB
        R1 = R0 + 64 * KIB
        R2 = R1 + 32 * KIB
        R3 = R2 + 64 * KIB
        RC = R3 + 48 * KIB

        def at(name, offset, shape, dt=F32):
            return nc.alloc_sbuf_tensor_at(name, [P, *shape], dt, offset=offset)

        hT_hi = at("hT_hi", R0, [KD, SEQ], F32R)
        hT_lo = at("hT_lo", R0 + 32 * KIB, [KD, SEQ], F32R)
        wout_hi = at("wout_hi", R0, [KD, D], F32R)
        wout_lo = at("wout_lo", R0 + 32 * KIB, [KD, D], F32R)
        act_hi = at("act_hi", R0, [2, 2, SEQ], F32R)
        act_lo = at("act_lo", R0 + 16 * KIB, [2, 2, SEQ], F32R)
        dn_hi = at("dn_hi", R0 + 32 * KIB, [2, D], F32R)
        dn_lo = at("dn_lo", R0 + 40 * KIB, [2, D], F32R)
        dn_raw = at("dn_raw", R0 + 48 * KIB, [2, D])
        silu_g = at("silu_g", R0 + 56 * KIB, [2, BANK])
        gated = at("gated", R0 + 60 * KIB, [2, BANK])

        x_in = at("x_in", R1, [NT, D])
        mixT = at("mixT", R1, [KD, SEQ])
        h2T_hi = at("h2T_hi", R1, [KD, SEQ], F32R)

        q_hi = at("q_hi", R2, [SEQ], F32R)
        q_lo = at("q_lo", R2 + 4 * KIB, [SEQ], F32R)
        k_hi = at("k_hi", R2 + 8 * KIB, [SEQ], F32R)
        k_lo = at("k_lo", R2 + 12 * KIB, [SEQ], F32R)
        v_hi = at("v_hi", R2 + 16 * KIB, [NT, P], F32R)
        v_lo = at("v_lo", R2 + 20 * KIB, [NT, P], F32R)
        vT = at("vT", R2 + 24 * KIB, [SEQ])
        prob = at("prob", R2 + 28 * KIB, [2, 2, SEQ])
        attT_hi = at("attT_hi", R2 + 44 * KIB, [NT, 2 * P], F32R)
        attT_lo = at("attT_lo", R2 + 52 * KIB, [NT, 2 * P], F32R)
        o_sq = at("o_sq", R2 + 60 * KIB, [2 * P])
        o_rstd = at("o_rstd", R2 + 61 * KIB, [2 * P])
        junk = at("junk", R2 + 24 * KIB, [D])
        xn = at("xn", R2 + 28 * KIB, [2, D])
        PAD = max(POOL_WINDOWS)
        win = [at(f"win{i}", R2 + (28 + 5 * i) * KIB, [PAD + SEQ]) for i in range(2)]
        resid = at("resid", R2 + 38 * KIB, [SEQ])
        res_hi = at("res_hi", R2 + 44 * KIB, [2, SEQ], F32R)
        res_lo = at("res_lo", R2 + 52 * KIB, [2, SEQ], F32R)
        x2 = at("x2", R2, [NT, D])
        h2T_lo = at("h2T_lo", R2 + 32 * KIB, [KD, SEQ], F32R)

        w_raw = at("w_raw", R3, [4, D])
        w_hi = at("w_hi", R3 + 16 * KIB, [4, D], F32R)
        w_lo = at("w_lo", R3 + 32 * KIB, [4, D], F32R)

        g1_row = at("g1_row", RC, [D])
        mask = at("mask", RC + 4 * KIB, [SEQ])
        xn2 = at("xn2", RC, [2, D])
        g2_row = at("g2_row", RC + 8 * KIB, [D])
        gf_row = at("gf_row", RC + 8 * KIB, [D])
        ident = at("ident", RC + 12 * KIB, [P])
        ones = at("ones", RC + 12 * KIB + 512, [P])
        lam_in = at("lam_in", R2, [4, HD])
        lam_pr = at("lam_pr", R2 + KIB, [2, HD])
        small = RC + 13 * KIB - 1536
        lam_sum = at("lam_sum", small + 1536, [2])
        lam_exp = at("lam_exp", small + 1568, [2])
        neg_lam = at("neg_lam", small + 1600, [2])
        subln_c = at("subln_c", small + 1632, [2])
        pscale_c = at("pscale_c", small + 1664, [G])
        inv_cnt = at("inv_cnt", small + 1696, [PAD])
        fix = at("fix", small + 1760, [PAD])
        eps_c = at("eps_c", small + 1824, [1])
        mhalf = at("mhalf", small + 1856, [NT])
        ss1 = at("ss1", small + 1888, [NT])
        rs1 = at("rs1", small + 1920, [NT])
        ss2 = at("ss2", small + 1952, [NT])
        rs2 = at("rs2", small + 1984, [NT])
        ss3 = at("ss3", small + 2016, [2 * NT])
        rs3 = at("rs3", small + 2080, [NT])
        smax = at("smax", small + 2112, [2, 2])
        nbias = at("nbias", small + 2144, [2, 2])
        lsum = at("lsum", small + 2176, [2, 2])
        rsum = at("rsum", small + 2208, [2, 2])
        ms = at("ms", small + 2240, [NT])

        PS = ctx.enter_context(nc.psum_tensor("PS", [P, 8, BANK], F32))

        def bank(b):
            return PS[:, b, :]

        def blocks(b, n=4):
            return PS[:, b, 0:n * P].rearrange("p (n c) -> p n c", c=P)

        x_in_here = [sem(f"x_in_here{i}") for i in range(NT // 2)]
        x2_here = [sem(f"x2_here{i}") for i in range(NT // 2)]
        small_here, g1_here, g2_here, gf_here = sem("small_here"), sem("g1_here"), sem("g2_here"), sem("gf_here")
        raw_here = [sem(f"raw_here{i}") for i in range(4)]
        dn_here = sem("dn_here")
        ident_set, mhalf_set, ones_set, eps_set, pads_set, mask_set, cnt_set = (
            sem("ident_set"), sem("mhalf_set"), sem("ones_set"), sem("eps_set"), sem("pads_set"),
            sem("mask_set"), sem("cnt_set"))
        dvec = sem("dvec")
        lam_ready, lam_a = sem("lam_ready"), sem("lam_a")
        sq1, pow1 = sem("sq1"), sem("pow1")
        poolc = sem("poolc")
        xn_ready = sem("xn_ready")
        tr1, tr1_hi, tr1_lo = sem("tr1"), sem("tr1_hi"), sem("tr1_lo")
        whi, wlo = sem("whi"), sem("wlo")
        u_mm, u_raw = sem("u_mm"), sem("u_raw")
        res_ready, res_hi_ready, res_lo_ready = sem("res_ready"), sem("res_hi_ready"), sem("res_lo_ready")
        y_mm, y_out = sem("y_mm"), sem("y_out")
        qk_mm, qk_hi, qk_lo = sem("qk_mm"), sem("qk_hi"), sem("qk_lo")
        v_mm, v_raw = sem("v_mm"), sem("v_raw")
        s_mm, s_read, nb_ready, exp_done, att_ready = (
            sem("s_mm"), sem("s_read"), sem("nb_ready"), sem("exp_done"), sem("att_ready"))
        t_mm, t_hi, t_lo = sem("t_mm"), sem("t_hi"), sem("t_lo")
        pv_mm, osq_ready, ss_mm, ln_done, rstd_ready, mix_ready = (
            sem("pv_mm"), sem("osq_ready"), sem("ss_mm"), sem("ln_done"), sem("rstd_ready"), sem("mix_ready"))
        mx_hi, mx_lo = sem("mx_hi"), sem("mx_lo")
        wo_hi, wo_lo = sem("wo_hi"), sem("wo_lo")
        o_mm, x2_add, sq2, pow2, xn2_ready = sem("o_mm"), sem("x2_add"), sem("sq2"), sem("pow2"), sem("xn2_ready")
        tr2, tr2_hi, tr2_lo = sem("tr2"), sem("tr2_hi"), sem("tr2_lo")
        fw_hi, fw_lo, fd_hi, fd_lo = sem("fw_hi"), sem("fw_lo"), sem("fd_hi"), sem("fd_lo")
        gu_mm, silu_done, gated_ready, act_hi_ready, act_ready = (
            sem("gu_mm"), sem("silu_done"), sem("gated_ready"), sem("act_hi_ready"), sem("act_ready"))
        d_mm = sem("d_mm")
        d_free = sem("d_free")
        sq3, pow3, y_ready, out_done = sem("sq3"), sem("pow3"), sem("y_ready"), sem("out_done")

        def blk_u(g):
            return g + 1
        BLK_PW = G + 1

        def blk_qkv(h, c):
            return G + 1 + 3 * h + c + 1
        BLKS = G + 1 + 3 * H

        def t_groups(qt):
            n = qt + 1
            return [("T", qt, k0, min(4, n - k0)) for k0 in range(0, n, 4)]
        T_OF_STEP = {2: t_groups(0), 3: t_groups(1) + [("V", 0, 0, 4)], 4: t_groups(2), 5: t_groups(3),
                     6: t_groups(4), 7: t_groups(5) + [("V", 1, 4, 4)], 8: t_groups(6), 9: t_groups(7)}
        T_ORDER = [g for s in range(2, 10) for g in T_OF_STEP[s]]
        T_PER_HEAD = len(T_ORDER)
        assert T_PER_HEAD % 2 == 0

        def t_index(h, group):
            return h * T_PER_HEAD + T_ORDER.index(group)

        def last_group(h, kind, n):
            return max(t_index(h, g) for g in T_ORDER if g[0] == kind and g[1] == n) + 1

        NPAIR = NT // 2
        WO_ORDER = list(range(H, KD)) + list(range(H))

        def wo_slot(n):
            return (n + 3) % 4

        block = ctx.enter_context(nc.Block())

        @block.sync
        def _(sp):
            xt = x[0].rearrange("(t p) d -> p t d", p=P)
            w_in_v = w_in[0].rearrange("(k p) n -> p k n", p=P)
            w_out_v = w_out[0].rearrange("(k p) n -> p k n", p=P)
            gate_v = w_gate[0].rearrange("(k p) n -> p k n", p=P)
            up_v = w_up[0].rearrange("(k p) n -> p k n", p=P)
            down_v = w_down[0].rearrange("(f p) n -> p f n", p=P)
            slot = [w_raw[:, c, :].rearrange("p (k n) -> p k n", k=KD) for c in range(4)]

            def load_x(i):
                sp.dma_start(x_in[:, 2 * i:2 * i + 2, :], xt[:, 2 * i:2 * i + 2, :]).then_inc(x_in_here[i], 16)

            def load_in(c, col):
                sp.dma_start(slot[c], w_in_v[:, :, col:col + P]).then_inc(raw_here[c], 16)

            load_x(0)
            sp.dma_start(g1_row[:, :], norm1_g[0:1, :].to_broadcast([P, D])).then_inc(g1_here, 16)
            load_x(1)
            load_in(0, 3 * ATTN)
            load_in(1, 3 * ATTN + P)
            load_x(2)
            load_in(2, 3 * ATTN + 2 * P)
            load_x(3)
            load_in(3, 3 * ATTN + 3 * P)
            sp.dma_start(lam_in[:, :, :], lam_qk[0:1, :, :].to_broadcast([P, 4, HD])).then_inc(small_here, 16)
            sp.dma_start(subln_c[:, 0:1], subln_g.rearrange("a (d b) -> (a d) b", b=1)).then_inc(small_here, 16)
            for g in range(G):
                sp.dma_start(pscale_c[:, g:g + 1], pool_scale[0].rearrange("(g p b) -> g p b", p=P, b=1)[g])\
                  .then_inc(small_here, 16)
            sp.dma_start(g2_row[:, :], norm2_g[0:1, :].to_broadcast([P, D])).then_inc(g2_here, 16)
            sp.wait_ge(wlo, blk_u(3))
            sp.dma_start(w_raw[:, 3, 0:G * P].rearrange("p (g n) -> p g n", g=G),
                         pool_w[0].rearrange("g c n -> c g n")).then_inc(raw_here[3], 16)
            for h in range(H):
                for c in range(3):
                    sp.wait_ge(wlo, blk_u(c) if h == 0 else blk_qkv(h - 1, c))
                    load_in(c, c * ATTN + h * P)
            for n, e in enumerate(WO_ORDER):
                if n == 0:
                    sp.wait_ge(wlo, BLK_PW)
                elif n < 4:
                    sp.wait_ge(wlo, blk_qkv(H - 1, wo_slot(n)))
                else:
                    sp.wait_ge(wo_lo, n - 3)
                sp.dma_start(w_raw[:, wo_slot(n), :], w_out_v[:, e, :]).then_inc(raw_here[wo_slot(n)], 16)
            sp.wait_ge(s_mm, H * NT)
            sp.wait_ge(pv_mm, H * NPAIR)
            sp.wait_ge(t_mm, H * T_PER_HEAD)
            for i in range(NT // 2):
                sp.dma_start(x2[:, 2 * i:2 * i + 2, :], xt[:, 2 * i:2 * i + 2, :]).then_inc(x2_here[i], 16)

            def load_gu(s, c, kind):
                src = (gate_v, up_v)[kind]
                cols = bass.ds(s * 2 * P + c * P, P) if not isinstance(s, int) else slice(s * 2 * P + c * P, s * 2 * P + c * P + P)
                sp.dma_start(slot[2 * c + kind], src[:, :, cols]).then_inc(raw_here[2 * c + kind], 16)

            for c in range(4):
                n = max(m for m in range(KD) if wo_slot(m) == c)
                sp.wait_ge(wo_lo, n + 1)
                load_gu(0, c // 2, c % 2)
            sp.wait_ge(o_mm, 4 * NPAIR)
            sp.dma_start(dn_raw[:, :, :], down_v[:, 0:2, :]).then_inc(dn_here, 16)
            sp.wait_ge(xn2_ready, NT)
            sp.dma_start(gf_row[:, :], final_g.rearrange("(a d) -> a d", a=1).to_broadcast([P, D])).then_inc(gf_here, 16)
            with nc.Fori(1, STEPS, engines=[ENG.SP]) as s:
                for c in range(4):
                    sp.wait_ge(fw_lo, s * 4 + (c - 3))
                    load_gu(s, c // 2, c % 2)
                sp.wait_ge(fd_lo, s)
                sp.dma_start(dn_raw[:, :, :], down_v[:, bass.ds(s * 2, 2), :]).then_inc(dn_here, 16)
            for t in range(NT):
                sp.wait_ge(y_ready, t + 1)
                sp.dma_start(out[0, t * P:(t + 1) * P, :], x2[:, t, :]).then_inc(out_done, 16)
            sp.wait_ge(out_done, 16 * NT)

        @block.gpsimd
        def _(gp):
            chain = [0]

            def link(ins):
                chain[0] += 1
                ins.then_inc(poolc, 1)
                gp.wait_ge(poolc, chain[0])

            link(nc.gpsimd.memset(ident[:, :], 0.0))
            nc.gpsimd.affine_select(out=ident[:, :], in_=ident[:, :], compare_op=ALU.not_equal, fill=1.0,
                                    base=0, pattern=[[-1, P]], channel_multiplier=1).then_inc(ident_set, 1)
            nc.gpsimd.memset(mhalf[:, :], -0.5).then_inc(mhalf_set, 1)
            gp.wait_ge(mhalf_set, 1)

            def low(c, n, width=D):
                gp.wait_ge(whi, n)
                nc.gpsimd.tensor_tensor(w_lo[:, c, 0:width], w_raw[:, c, 0:width], w_hi[:, c, 0:width].bitcast(F32),
                                        ALU.subtract).then_inc(wlo, 1)

            for t in range(NT):
                if t == 4:
                    low(0, blk_u(0))
                    low(1, blk_u(1))
                gp.wait_ge(sq1, t + 1)
                link(nc.gpsimd.tensor_scalar(ms[:, t:t + 1], ss1[:, t:t + 1], 1.0 / D, NORM_EPS, ALU.mult, ALU.add))
                nc.gpsimd.tensor_tensor(rs1[:, t:t + 1], ms[:, t:t + 1], mhalf[:, 0:1], ALU.pow).then_inc(pow1, 1)
            low(2, blk_u(2))
            low(3, blk_u(3))
            nc.gpsimd.memset(ones[:, :], 1.0).then_inc(ones_set, 1)
            nc.gpsimd.memset(eps_c[:, :], NORM_EPS).then_inc(eps_set, 1)
            gp.wait_ge(tr1, 2 * NT)
            for i in range(2):
                nc.gpsimd.memset(win[i][:, 0:PAD], 0.0).then_inc(pads_set, 1)
            for j in range(PAD):
                nc.gpsimd.memset(inv_cnt[:, j:j + 1], 1.0 / (j + 1)).then_inc(cnt_set, 1)
            low(3, BLK_PW, G * P)
            link(nc.gpsimd.memset(mask[:, :], 0.0))
            nc.gpsimd.affine_select(out=mask[:, SEQ - P:SEQ], in_=mask[:, SEQ - P:SEQ], compare_op=ALU.is_ge,
                                    fill=MASKED, base=0, pattern=[[-1, P]], channel_multiplier=1).then_inc(mask_set, 1)
            for h in range(H):
                for c in range(3):
                    low(c, blk_qkv(h, c), D)
            for n, e in enumerate(WO_ORDER):
                gp.wait_ge(wo_hi, n + 1)
                nc.gpsimd.tensor_tensor(wout_lo[:, e, :], w_raw[:, wo_slot(n), :], wout_hi[:, e, :].bitcast(F32),
                                        ALU.subtract).then_inc(wo_lo, 1)

            def pow_x2(t):
                gp.wait_ge(sq2, t + 1)
                link(nc.gpsimd.tensor_scalar(ms[:, t:t + 1], ss2[:, t:t + 1], 1.0 / D, NORM_EPS, ALU.mult, ALU.add))
                nc.gpsimd.tensor_tensor(rs2[:, t:t + 1], ms[:, t:t + 1], mhalf[:, 0:1], ALU.pow).then_inc(pow2, 1)

            def low_gu(s, c):
                gp.wait_ge(fw_hi, s * 4 + c + 1)
                nc.gpsimd.tensor_tensor(w_lo[:, c, :], w_raw[:, c, :], w_hi[:, c, :].bitcast(F32),
                                        ALU.subtract).then_inc(fw_lo, 1)

            def low_dn(s):
                gp.wait_ge(fd_hi, s + 1)
                nc.gpsimd.tensor_tensor(dn_lo[:, :, :], dn_raw[:, :, :], dn_hi[:, :, :].bitcast(F32),
                                        ALU.subtract).then_inc(fd_lo, 1)

            for t in range(NT - 2):
                pow_x2(t)
            low_gu(0, 0)
            low_gu(0, 1)
            pow_x2(NT - 2)
            pow_x2(NT - 1)
            low_gu(0, 2)
            low_gu(0, 3)
            with nc.Fori(1, STEPS, engines=[ENG.Pool]) as s:
                for c in range(4):
                    low_gu(s, c)
                low_dn(s - 1)
            low_dn(STEPS - 1)
            for t in range(NT):
                gp.wait_ge(sq3, 2 * t + 2)
                link(nc.gpsimd.tensor_tensor(ms[:, t:t + 1], ss3[:, 2 * t:2 * t + 1], ss3[:, 2 * t + 1:2 * t + 2], ALU.add))
                link(nc.gpsimd.tensor_scalar(ms[:, t:t + 1], ms[:, t:t + 1], 1.0 / D, NORM_EPS, ALU.mult, ALU.add))
                nc.gpsimd.tensor_tensor(rs3[:, t:t + 1], ms[:, t:t + 1], mhalf[:, 0:1], ALU.pow).then_inc(pow3, 1)

        @block.scalar
        def _(act):
            nc.scalar.preload_act_table_set("natural_log_exp_and_others")

            def split_hi(c, n, count, width=D):
                act.wait_ge(raw_here[c], 16 * count)
                nc.scalar.copy(w_hi[:, c, 0:width], w_raw[:, c, 0:width]).then_inc(whi, 1)

            def hi_x(t):
                for j in range(2):
                    act.wait_ge(tr1, 2 * t + j + 1)
                    nc.scalar.copy(hT_hi[:, 4 * j:4 * j + 4, t * P:(t + 1) * P], blocks(4 + j)).then_inc(tr1_hi, 1)

            def square_x(t):
                act.wait_ge(x_in_here[t // 2], 16)
                if t:
                    act.wait_ge(sq1, t)
                nc.scalar.activation(junk[:, :], x_in[:, t, :], ACT.Square, accum_out=ss1[:, t:t + 1]).then_inc(sq1, 1)

            for t in range(NT):
                if t == 4:
                    split_hi(0, blk_u(0), 1)
                    hi_x(3)
                    split_hi(1, blk_u(1), 1)
                if t == 6:
                    split_hi(2, blk_u(2), 1)
                square_x(t)
                if t and t != 4:
                    hi_x(t - 1)
            hi_x(NT - 1)
            split_hi(3, blk_u(3), 1)

            act.wait_ge(xn_ready, NT)
            for n in range(2 * G):
                half, g = divmod(n, G)
                act.wait_ge(u_mm, n + 1)
                nc.scalar.copy(mixT[:, H + g, half * HALF:(half + 1) * HALF], bank(n % 4)).then_inc(u_raw, 1)
            split_hi(3, BLK_PW, 2, G * P)
            for c in range(3):
                split_hi(c, blk_qkv(0, c), 2)
            act.wait_ge(lam_ready, 1)
            nc.scalar.activation(lam_exp[:, :], lam_sum[:, :], ACT.Exp).then_inc(lam_a, 1)

            def res_high(g):
                act.wait_ge(res_ready, g + 1)
                if g >= 2:
                    act.wait_ge(y_mm, 2 * (g - 1))
                nc.scalar.copy(res_hi[:, g % 2, :], resid[:, :]).then_inc(res_hi_ready, 1)

            def y_evac(g):
                for half in range(2):
                    act.wait_ge(y_mm, 2 * g + half + 1)
                    nc.scalar.activation(mixT[:, H + g, half * HALF:(half + 1) * HALF], bank((6, 1)[half]),
                                         ACT.Copy, scale=pscale_c[:, g:g + 1]).then_inc(y_out, 1)

            def qk_high(h, n):
                act.wait_ge(qk_mm, 4 * h + n + 1)
                dst = (q_hi, k_hi)[n % 2]
                nc.scalar.copy(dst[:, (n // 2) * HALF:(n // 2 + 1) * HALF], bank((0, 2, 3, 7)[n])).then_inc(qk_hi, 1)

            def v_copy(h, half):
                act.wait_ge(v_mm, 2 * h + half + 1)
                if h:
                    act.wait_ge(t_mm, last_group(h - 1, "V", half))
                nc.scalar.copy(vT[:, half * HALF:(half + 1) * HALF], bank(7)).then_inc(v_raw, 1)

            def t_high(h, group):
                kind, n, k0, nb = group
                i = t_index(h, group)
                act.wait_ge(t_mm, i + 1)
                if kind == "V":
                    if h:
                        act.wait_ge(pv_mm, NPAIR * h)
                    dst = v_hi[:, k0:k0 + nb, :]
                else:
                    done = NPAIR * h + n // 2
                    if done:
                        act.wait_ge(pv_mm, done)
                    dst = attT_hi[:, k0:k0 + nb, (n % 2) * P:(n % 2 + 1) * P]
                nc.scalar.copy(dst, blocks(4 + i % 2, nb)).then_inc(t_hi, 1)

            def exps(h, s):
                n = NT * h + s
                L = (s + 1) * P
                act.wait_ge(nb_ready, n + 1)
                for r in range(2):
                    nc.scalar.activation(prob[:, s % 2, r, 0:L], prob[:, s % 2, r, 0:L], ACT.Exp,
                                         bias=nbias[:, s % 2, r:r + 1], scale=SCALE,
                                         accum_out=lsum[:, s % 2, r:r + 1]).then_inc(exp_done, 1)

            def o_square(h, j):
                n = NPAIR * h + j
                act.wait_ge(pv_mm, n + 1)
                if n:
                    act.wait_ge(ss_mm, n)
                nc.scalar.activation(o_sq[:, :], PS[:, 6, 0:2 * P], ACT.Square).then_inc(osq_ready, 1)

            def o_rsqrt(h, j):
                n = NPAIR * h + j
                act.wait_ge(ss_mm, n + 1)
                if n:
                    act.wait_ge(mix_ready, n)
                nc.scalar.activation(o_rstd[:, :], PS[:, 6, 2 * P:4 * P], ACT.Ln, bias=eps_c[:, 0:1],
                                     scale=1.0 / VD).then_inc(ln_done, 1)
                act.wait_ge(ln_done, n + 1)
                nc.scalar.activation(o_rstd[:, :], o_rstd[:, :], ACT.Exp, scale=-0.5).then_inc(rstd_ready, 1)

            def wout_high(n):
                e, c = WO_ORDER[n], wo_slot(n)
                count = (2 if c == 3 else 1 + H) + 1 + (n >= 4)
                if n == 0:
                    act.wait_ge(v_mm, 2 * H)
                act.wait_ge(raw_here[c], 16 * count)
                nc.scalar.copy(wout_hi[:, e, :], w_raw[:, c, :]).then_inc(wo_hi, 1)

            act.wait_ge(eps_set, 1)
            res_high(0)
            for h in range(H):
                qk_high(h, 0)
                if h:
                    for g in T_OF_STEP[8]:
                        t_high(h - 1, g)
                    o_square(h - 1, 2)
                else:
                    res_high(1)
                    y_evac(0)
                qk_high(h, 1)
                if h:
                    for g in T_OF_STEP[9]:
                        t_high(h - 1, g)
                    o_rsqrt(h - 1, 2)
                else:
                    res_high(2)
                    y_evac(1)
                    res_high(3)
                for s in range(NT):
                    for g in T_OF_STEP.get(s, []):
                        if g[0] == "T":
                            t_high(h, g)
                    exps(h, s)
                    if s == 0:
                        v_copy(h, 0)
                        if h:
                            o_square(h - 1, 3)
                        else:
                            y_evac(2)
                    if s == 1:
                        qk_high(h, 2)
                        if h:
                            o_rsqrt(h - 1, 3)
                        else:
                            y_evac(3)
                    if s == 2:
                        qk_high(h, 3)
                    if s in (4, 6):
                        o_square(h, (s - 4) // 2)
                    if s == 6:
                        v_copy(h, 1)
                    if s in (5, 7):
                        o_rsqrt(h, (s - 5) // 2)
                    for g in T_OF_STEP.get(s, []):
                        if g[0] == "V":
                            t_high(h, g)
                    if h + 1 < H and s in (3, 4):
                        c = s - 3
                        act.wait_ge(qk_mm, 4 * h + 4)
                        split_hi(c, blk_qkv(h + 1, c), 3 + h)
                    if h + 1 < H and s == 7:
                        act.wait_ge(v_mm, 2 * h + 2)
                        split_hi(2, blk_qkv(h + 1, 2), 3 + h)
            h = H - 1

            def mix_high(t):
                if t == 0:
                    act.wait_ge(qk_mm, 4 * H)
                if t == 2:
                    act.wait_ge(v_mm, 2 * H)
                act.wait_ge(mix_ready, NPAIR * (H - 1) + t // 2 + 1)
                if t >= 4:
                    act.wait_ge(o_mm, 4 * (t // 2 - 1))
                nc.scalar.copy(w_hi[:, t % 4, :].rearrange("p (e n) -> p e n", e=KD),
                               mixT[:, :, t * P:(t + 1) * P]).then_inc(mx_hi, 1)

            mix_high(0)
            mix_high(1)
            wout_high(0)
            wout_high(1)
            for g in T_OF_STEP[8]:
                t_high(h, g)
            o_square(h, 2)
            wout_high(2)
            for g in T_OF_STEP[9]:
                t_high(h, g)
            o_rsqrt(h, 2)
            wout_high(3)
            o_square(h, 3)
            wout_high(4)
            wout_high(5)
            o_rsqrt(h, 3)
            wout_high(6)
            wout_high(7)
            mix_high(2)
            mix_high(3)

            def square_x2(t):
                act.wait_ge(x2_add, 2 * t + 2)
                if t >= 2:
                    act.wait_ge(tr2, 2 * (t - 1))
                nc.scalar.activation(xn2[:, t % 2, :], x2[:, t, :], ACT.Square, accum_out=ss2[:, t:t + 1]).then_inc(sq2, 1)

            def hi_x2(t):
                for j in range(2):
                    act.wait_ge(tr2, 2 * t + j + 1)
                    act.wait_ge(mx_lo, t + 1)
                    nc.scalar.copy(h2T_hi[:, 4 * j:4 * j + 4, t * P:(t + 1) * P],
                                   blocks(4 * ((t // 2) % 2) + 2 * (t % 2) + j)).then_inc(tr2_hi, 1)

            def gu_high(s, c):
                act.wait_ge(raw_here[c], (s + FIRST_GU[c]) * 16)
                nc.scalar.copy(w_hi[:, c, :], w_raw[:, c, :]).then_inc(fw_hi, 1)

            def dn_high(s):
                act.wait_ge(dn_here, s * 16 + 16)
                nc.scalar.copy(dn_hi[:, :, :], dn_raw[:, :, :]).then_inc(fd_hi, 1)

            FIRST_GU = [1 + H + sum(wo_slot(n) == c for n in range(KD)) + 1 for c in range(3)] \
                + [2 + sum(wo_slot(n) == 3 for n in range(KD)) + 1]

            for p in range(NPAIR):
                square_x2(2 * p)
                square_x2(2 * p + 1)
                if p + 2 < NPAIR:
                    mix_high(2 * p + 4)
                    mix_high(2 * p + 5)
                if p == 2:
                    gu_high(0, 0)
                    gu_high(0, 1)
                if p < NPAIR - 1:
                    hi_x2(2 * p)
                    hi_x2(2 * p + 1)

            def gate_up(s, c, half, slot):
                n = 2 * c + half
                act.wait_ge(gu_mm, s * 8 + 2 * n + 1)
                if not (isinstance(s, int) and s == 0 and n < 2):
                    act.wait_ge(gated_ready, s * 4 + n - 1)
                nc.scalar.activation(silu_g[:, n % 2, :], bank(2 * half), ACT.Silu).then_inc(silu_done, 1)
                act.wait_ge(gated_ready, s * 4 + n + 1)
                nc.scalar.copy(act_hi[:, slot, c, half * HALF:(half + 1) * HALF], gated[:, n % 2, :]).then_inc(act_hi_ready, 1)

            def ff_act(s, slot, first=False, last=False):
                for c in range(2):
                    for half in range(2):
                        gate_up(s, c, half, slot)
                        if first and c == 0 and half == 0:
                            hi_x2(NT - 2)
                            hi_x2(NT - 1)
                            gu_high(0, 2)
                            gu_high(0, 3)
                    if not last:
                        act.wait_ge(gu_mm, s * 8 + (4 * c + 4))
                        gu_high(s + 1, 2 * c)
                        gu_high(s + 1, 2 * c + 1)
                if not first:
                    act.wait_ge(d_mm, s * 16)
                dn_high(s)

            act.wait_ge(o_mm, 4 * NPAIR)
            ff_act(0, 0, first=True)
            with nc.Fori(0, STEPS // 2 - 1, engines=[ENG.Activation]) as i:
                ff_act(i * 2 + 1, 1)
                ff_act(i * 2 + 2, 0)
            ff_act(STEPS - 2, 1)
            ff_act(STEPS - 1, 0, last=True)

            for t in range(NT):
                for half in range(2):
                    act.wait_ge(d_free, 4 + 16 * (STEPS - 1) + 2 * t + half + 1)
                    n = 2 * t + half
                    if n >= 2:
                        act.wait_ge(sq3, n - 1)
                    nc.scalar.activation(gated[:, n % 2, :], x2[:, t, half * BANK:(half + 1) * BANK], ACT.Square,
                                         accum_out=ss3[:, n:n + 1]).then_inc(sq3, 1)

        @block.vector
        def _(ve):
            chain = [0]

            def link(ins):
                chain[0] += 1
                ins.then_inc(dvec, 1)
                ve.wait_ge(dvec, chain[0])

            def x_norm(t):
                ve.wait_ge(x_in_here[t // 2], 16)
                ve.wait_ge(pow1, t + 1)
                if t >= 2:
                    ve.wait_ge(tr1, 2 * t - 2)
                nc.vector.scalar_tensor_tensor(out=xn[:, t % 2, :], in0=x_in[:, t, :], scalar=rs1[:, t:t + 1],
                                               in1=g1_row[:, :], op0=ALU.mult, op1=ALU.mult).then_inc(xn_ready, 1)

            def lo_x(t):
                for j in range(2):
                    ve.wait_ge(tr1_hi, 2 * t + j + 1)
                    cols = slice(t * P, (t + 1) * P)
                    nc.vector.tensor_tensor(hT_lo[:, 4 * j:4 * j + 4, cols], blocks(4 + j),
                                            hT_hi[:, 4 * j:4 * j + 4, cols].bitcast(F32),
                                            ALU.subtract).then_inc(tr1_lo, 1)

            ve.wait_ge(g1_here, 16)
            for t in range(NT):
                x_norm(t)
                if t:
                    lo_x(t - 1)
            lo_x(NT - 1)

            ve.wait_ge(small_here, 16 * (2 + G))
            for r in range(2):
                link(nc.vector.tensor_tensor(lam_pr[:, r, :], lam_in[:, 2 * r, :], lam_in[:, 2 * r + 1, :], ALU.mult))
                nc.vector.reduce_sum(lam_sum[:, r:r + 1], lam_pr[:, r, :], mybir.AxisListType.X).then_inc(dvec, 1)
                chain[0] += 1
            ve.wait_ge(dvec, chain[0])
            link(nc.vector.tensor_scalar(subln_c[:, 1:2], subln_c[:, 0:1], 1.0 - LAMBDA_INIT, None, ALU.mult))
            nc.vector.memset(fix[:, :], 0.0).then_inc(lam_ready, 1)

            def pooling(g):
                w = POOL_WINDOWS[g]
                u = mixT[:, H + g, :]
                ve.wait_ge(u_raw, G + g + 1)
                link(nc.vector.tensor_copy(win[0][:, PAD:PAD + 1], u[:, 0:1]))
                link(nc.vector.tensor_tensor(win[0][:, PAD + 1:PAD + SEQ], u[:, 1:SEQ], u[:, 0:SEQ - 1], ALU.add))
                a, reach = 0, 2
                while reach < w:
                    link(nc.vector.tensor_tensor(win[1 - a][:, PAD:PAD + SEQ], win[a][:, PAD:PAD + SEQ],
                                                 win[a][:, PAD - reach:PAD + SEQ - reach], ALU.add))
                    a, reach = 1 - a, 2 * reach
                link(nc.vector.tensor_tensor(fix[:, 0:w - 1], win[a][:, PAD:PAD + w - 1], inv_cnt[:, 0:w - 1], ALU.mult))
                link(nc.vector.tensor_tensor(resid[:, 0:w - 1], fix[:, 0:w - 1], u[:, 0:w - 1], ALU.subtract))
                nc.vector.scalar_tensor_tensor(out=resid[:, w - 1:SEQ], in0=win[a][:, PAD + w - 1:PAD + SEQ],
                                               scalar=1.0 / w, in1=u[:, w - 1:SEQ], op0=ALU.mult,
                                               op1=ALU.subtract).then_inc(res_ready, 1)
                ve.wait_ge(res_ready, g + 1)
                ve.wait_ge(res_hi_ready, g + 1)
                nc.vector.tensor_tensor(res_lo[:, g % 2, :], resid[:, :], res_hi[:, g % 2, :].bitcast(F32),
                                        ALU.subtract).then_inc(res_lo_ready, 1)
                ve.wait_ge(res_lo_ready, g + 1)

            def qk_low(h, n):
                ve.wait_ge(qk_hi, 4 * h + n + 1)
                hi, lo = ((q_hi, q_lo), (k_hi, k_lo))[n % 2]
                cols = slice((n // 2) * HALF, (n // 2 + 1) * HALF)
                nc.vector.tensor_tensor(lo[:, cols], bank((0, 2, 3, 7)[n]), hi[:, cols].bitcast(F32),
                                        ALU.subtract).then_inc(qk_lo, 1)

            def t_low(h, group):
                kind, n, k0, nb = group
                i = t_index(h, group)
                ve.wait_ge(t_hi, i + 1)
                if kind == "V":
                    lo, hi = v_lo[:, k0:k0 + nb, :], v_hi[:, k0:k0 + nb, :]
                else:
                    cols = slice((n % 2) * P, (n % 2 + 1) * P)
                    lo, hi = attT_lo[:, k0:k0 + nb, cols], attT_hi[:, k0:k0 + nb, cols]
                nc.vector.tensor_tensor(lo, blocks(4 + i % 2, nb), hi.bitcast(F32), ALU.subtract).then_inc(t_lo, 1)

            def mask_max(h, s):
                n = NT * h + s
                L = (s + 1) * P
                ve.wait_ge(s_mm, n + 1)
                if n >= 2:
                    ve.wait_ge(t_mm, last_group(h, "T", s - 2) if s >= 2 else last_group(h - 1, "T", NT + s - 2))
                for r in range(2):
                    nc.vector.tensor_tensor_reduce(
                        out=prob[:, s % 2, r, 0:L],
                        in0=PS[:, 2 * r:2 * r + 2, :].rearrange("p b n -> p (b n)")[:, 0:L],
                        in1=mask[:, SEQ - L:SEQ], scale=1.0, scalar=LOWEST, op0=ALU.add, op1=ALU.max,
                        accum_out=smax[:, s % 2, r:r + 1]).then_inc(s_read, 1)
                ve.wait_ge(s_read, 2 * n + 2)
                nc.vector.tensor_scalar(nbias[:, s % 2, :], smax[:, s % 2, :], -SCALE, None, ALU.mult).then_inc(nb_ready, 1)

            def combine(h, s):
                n = NT * h + s
                L = (s + 1) * P
                ve.wait_ge(exp_done, 2 * n + 2)
                link(nc.vector.reciprocal(rsum[:, s % 2, :], lsum[:, s % 2, :]))
                link(nc.vector.tensor_scalar(prob[:, s % 2, 1, 0:L], prob[:, s % 2, 1, 0:L], rsum[:, s % 2, 1:2],
                                             neg_lam[:, 0:1], ALU.mult, ALU.mult))
                nc.vector.scalar_tensor_tensor(out=prob[:, s % 2, 0, 0:L], in0=prob[:, s % 2, 0, 0:L],
                                               scalar=rsum[:, s % 2, 0:1], in1=prob[:, s % 2, 1, 0:L],
                                               op0=ALU.mult, op1=ALU.add).then_inc(att_ready, 1)

            def o_norm(h, j):
                n = NPAIR * h + j
                ve.wait_ge(rstd_ready, n + 1)
                nc.vector.scalar_tensor_tensor(out=mixT[:, h, j * 2 * P:(j + 1) * 2 * P], in0=PS[:, 6, 0:2 * P],
                                               scalar=subln_c[:, 1:2], in1=o_rstd[:, :], op0=ALU.mult,
                                               op1=ALU.mult).then_inc(mix_ready, 1)

            ve.wait_ge(pads_set, 2)
            ve.wait_ge(cnt_set, PAD)
            for g in range(G - 1):
                pooling(g)
            ve.wait_ge(lam_a, 1)
            link(nc.vector.tensor_scalar(neg_lam[:, 1:2], lam_exp[:, 1:2], -LAMBDA_INIT, None, ALU.add))
            link(nc.vector.tensor_tensor(neg_lam[:, 0:1], neg_lam[:, 1:2], lam_exp[:, 0:1], ALU.subtract))
            ve.wait_ge(mask_set, 1)
            for h in range(H):
                if h:
                    combine(h - 1, NT - 1)
                qk_low(h, 0)
                if h:
                    for g in T_OF_STEP[8]:
                        t_low(h - 1, g)
                else:
                    pooling(G - 1)
                qk_low(h, 1)
                if h:
                    for g in T_OF_STEP[9]:
                        t_low(h - 1, g)
                    o_norm(h - 1, 2)
                for s in range(NT):
                    mask_max(h, s)
                    if s:
                        combine(h, s - 1)
                    if s == 1:
                        qk_low(h, 2)
                        if h:
                            o_norm(h - 1, 3)
                    if s == 2:
                        qk_low(h, 3)
                    if s in (5, 7):
                        o_norm(h, (s - 5) // 2)
                    for g in T_OF_STEP.get(s, []):
                        t_low(h, g)

            def mix_low(t):
                ve.wait_ge(mx_hi, t + 1)
                nc.vector.tensor_tensor(w_lo[:, t % 4, :].rearrange("p (e n) -> p e n", e=KD),
                                        mixT[:, :, t * P:(t + 1) * P],
                                        w_hi[:, t % 4, :].bitcast(F32).rearrange("p (e n) -> p e n", e=KD),
                                        ALU.subtract).then_inc(mx_lo, 1)

            h = H - 1
            mix_low(0)
            mix_low(1)
            combine(h, NT - 1)
            for g in T_OF_STEP[8] + T_OF_STEP[9]:
                t_low(h, g)
            o_norm(h, 2)
            o_norm(h, 3)
            mix_low(2)
            mix_low(3)

            def x2_norm(t):
                ve.wait_ge(pow2, t + 1)
                nc.vector.scalar_tensor_tensor(out=xn2[:, t % 2, :], in0=x2[:, t, :], scalar=rs2[:, t:t + 1],
                                               in1=g2_row[:, :], op0=ALU.mult, op1=ALU.mult).then_inc(xn2_ready, 1)

            def lo_x2(t):
                for j in range(2):
                    ve.wait_ge(tr2_hi, 2 * t + j + 1)
                    cols = slice(t * P, (t + 1) * P)
                    nc.vector.tensor_tensor(h2T_lo[:, 4 * j:4 * j + 4, cols],
                                            blocks(4 * ((t // 2) % 2) + 2 * (t % 2) + j),
                                            h2T_hi[:, 4 * j:4 * j + 4, cols].bitcast(F32),
                                            ALU.subtract).then_inc(tr2_lo if t < NT - 2 else d_free, 1)

            ve.wait_ge(g2_here, 16)
            for p in range(NPAIR):
                ve.wait_ge(x2_here[p], 16)
                for i in range(2):
                    for half in range(2):
                        t = 2 * p + i
                        cols = slice(half * BANK, (half + 1) * BANK)
                        ve.wait_ge(o_mm, 2 * t + half + 1)
                        nc.vector.tensor_tensor(x2[:, t, cols], bank(4 * (p % 2) + 2 * i + half), x2[:, t, cols],
                                                ALU.add).then_inc(x2_add, 1)
                if p + 2 < NPAIR:
                    mix_low(2 * p + 4)
                    mix_low(2 * p + 5)
                x2_norm(2 * p)
                x2_norm(2 * p + 1)
                if p < NPAIR - 1:
                    lo_x2(2 * p)
                    lo_x2(2 * p + 1)

            def gate_up(s, c, half, slot):
                n = 2 * c + half
                ve.wait_ge(gu_mm, s * 8 + (2 * n + 2))
                ve.wait_ge(silu_done, s * 4 + (n + 1))
                nc.vector.tensor_tensor(gated[:, n % 2, :], silu_g[:, n % 2, :], bank(2 * half + 1),
                                        ALU.mult).then_inc(gated_ready, 1)
                ve.wait_ge(act_hi_ready, s * 4 + (n + 1))
                cols = slice(half * HALF, (half + 1) * HALF)
                nc.vector.tensor_tensor(act_lo[:, slot, c, cols], gated[:, n % 2, :],
                                        act_hi[:, slot, c, cols].bitcast(F32), ALU.subtract).then_inc(act_ready, 1)

            def add_down(s, t, half):
                n = 2 * t + half
                cols = slice(half * BANK, (half + 1) * BANK)
                ve.wait_ge(d_mm, s * 16 + (n + 1))
                nc.vector.tensor_tensor(x2[:, t, cols], bank(4 + n % 4), x2[:, t, cols], ALU.add).then_inc(d_free, 1)

            def ff_gate(s, slot, first=False):
                for c in range(2):
                    for half in range(2):
                        gate_up(s, c, half, slot)
                        if first and c == 0 and half == 0:
                            lo_x2(NT - 2)
                            lo_x2(NT - 1)

            def ff_down(s):
                for t in range(NT):
                    for half in range(2):
                        add_down(s, t, half)

            ff_gate(0, 0, first=True)
            with nc.Fori(0, STEPS // 2 - 1, engines=[ENG.DVE]) as i:
                ff_gate(i * 2 + 1, 1)
                ff_down(i * 2)
                ff_gate(i * 2 + 2, 0)
                ff_down(i * 2 + 1)
            ff_gate(STEPS - 2, 1)
            ff_down(STEPS - 3)
            ff_gate(STEPS - 1, 0)
            ff_down(STEPS - 2)

            def y_norm(t):
                ve.wait_ge(pow3, t + 1)
                nc.vector.scalar_tensor_tensor(out=x2[:, t, :], in0=x2[:, t, :], scalar=rs3[:, t:t + 1],
                                               in1=gf_row[:, :], op0=ALU.mult, op1=ALU.mult).then_inc(y_ready, 1)

            ve.wait_ge(gf_here, 16)
            for t in range(NT):
                for half in range(2):
                    add_down(STEPS - 1, t, half)
                if t >= 2:
                    y_norm(t - 2)
            y_norm(NT - 2)
            y_norm(NT - 1)

        @block.tensor
        def _(pe):
            def three(dst, a_hi, a_lo, b_hi, b_lo, start, stop):
                nc.tensor.matmul(dst, a_hi, b_hi, start=start, stop=False)
                nc.tensor.matmul(dst, a_hi, b_lo, start=False, stop=False)
                return nc.tensor.matmul(dst, a_lo, b_hi, start=False, stop=stop)

            def project(b, c, half, k0=0, k1=KD):
                for k in range(k0, k1):
                    ws = slice(k * P, (k + 1) * P)
                    cols = slice(half * HALF, (half + 1) * HALF)
                    mm = three(bank(b), w_hi[:, c, ws], w_lo[:, c, ws], hT_hi[:, k, cols], hT_lo[:, k, cols],
                               k == 0, k == KD - 1)
                return mm

            def x_tile(t):
                pe.wait_ge(xn_ready, t + 1)
                for j in range(2):
                    if t:
                        pe.wait_ge(tr1_lo, 2 * t + j - 1)
                    for k in range(4):
                        kk = 4 * j + k
                        tr = nc.tensor.transpose(bank(4 + j)[:, k * P:(k + 1) * P], xn[:, t % 2, kk * P:(kk + 1) * P],
                                                 ident[:, :])
                    tr.then_inc(tr1, 1)

            def u_group(n):
                half, g = divmod(n, G)
                if half == 0:
                    pe.wait_ge(wlo, blk_u(g))
                if n >= 4:
                    pe.wait_ge(u_raw, n - 3)
                project(n % 4, g, half).then_inc(u_mm, 1)

            pe.wait_ge(ident_set, 1)
            for t in range(4):
                x_tile(t)
            pe.wait_ge(tr1_lo, 8)
            u_group(0)
            x_tile(4)
            u_group(1)
            x_tile(5)
            u_group(2)
            x_tile(6)
            x_tile(7)
            u_group(3)
            pe.wait_ge(tr1_lo, 2 * NT)
            for n in range(4, 8):
                u_group(n)

            def y_group(g):
                if g == 0:
                    pe.wait_ge(wlo, BLK_PW)
                pe.wait_ge(res_lo_ready, g + 1)
                for half in range(2):
                    if g:
                        pe.wait_ge(y_out, 2 * g - 1 + half)
                    cols = slice(half * HALF, (half + 1) * HALF)
                    ws = slice(g * P, (g + 1) * P)
                    three(bank((6, 1)[half]), w_hi[:, 3, ws], w_lo[:, 3, ws], res_hi[:, g % 2, cols],
                          res_lo[:, g % 2, cols], True, True).then_inc(y_mm, 1)

            def qk_group(h, n):
                if n < 2:
                    pe.wait_ge(wlo, blk_qkv(h, n))
                    if h:
                        pe.wait_ge(s_read, 2 * NT * h)
                    else:
                        pe.wait_ge(u_raw, 2 * G)
                if n == 3:
                    pe.wait_ge(v_raw, 2 * h + 1)
                project((0, 2, 3, 7)[n], n % 2, n // 2).then_inc(qk_mm, 1)

            def v_part(h, half, k0, k1):
                if k0 == 0:
                    if half == 0:
                        pe.wait_ge(wlo, blk_qkv(h, 2))
                        if h:
                            pe.wait_ge(v_raw, 2 * h)
                    else:
                        pe.wait_ge(qk_lo, 4 * h + 4)
                mm = project(7, 2, half, k0, k1)
                if k1 == KD:
                    mm.then_inc(v_mm, 1)

            def scores(h, s):
                n = NT * h + s
                L = (s + 1) * P
                if n:
                    pe.wait_ge(s_read, 2 * n)
                if s == 0:
                    pe.wait_ge(qk_lo, 4 * h + 2)
                if s == 4:
                    pe.wait_ge(qk_lo, 4 * h + 4)
                    if h == 0:
                        pe.wait_ge(y_out, 2 * G)
                qs = slice(s * P, (s + 1) * P)
                for k0 in range(0, L, BANK):
                    w = min(BANK, L - k0)
                    ks = slice(k0, k0 + w)
                    for a, b, first, last in ((q_hi, k_hi, True, False), (q_hi, k_lo, False, False),
                                              (q_lo, k_hi, False, True)):
                        for r in range(2):
                            rows = slice(r * HD, (r + 1) * HD)
                            mm = nc.tensor.matmul(PS[:, 2 * r + k0 // BANK, 0:w], a[rows, qs], b[rows, ks],
                                                  start=first, stop=last)
                mm.then_inc(s_mm, 1)

            def transposes(h, group):
                kind, n, k0, nb = group
                i = t_index(h, group)
                if i >= 2:
                    pe.wait_ge(t_lo, i - 1)
                if kind == "V":
                    pe.wait_ge(v_raw, 2 * h + n + 1)
                else:
                    pe.wait_ge(att_ready, NT * h + n + 1)
                for b in range(nb):
                    kb = k0 + b
                    ks = slice(kb * P, (kb + 1) * P)
                    src = vT[:, ks] if kind == "V" else prob[:, n % 2, 0, ks]
                    tr = nc.tensor.transpose(bank(4 + i % 2)[:, b * P:(b + 1) * P], src, ident[:, :])
                tr.then_inc(t_mm, 1)

            def values(h, j):
                n = NPAIR * h + j
                if n:
                    pe.wait_ge(mix_ready, n)
                else:
                    pe.wait_ge(y_out, 2 * G)
                pe.wait_ge(t_lo, max(last_group(h, "T", 2 * j + 1), last_group(h, "V", 1 if j >= 2 else 0)))
                for kb in range(2 * j + 2):
                    c0 = 0 if kb <= 2 * j else P
                    mm = three(PS[:, 6, c0:2 * P], v_hi[:, kb, :], v_lo[:, kb, :], attT_hi[:, kb, c0:2 * P],
                               attT_lo[:, kb, c0:2 * P], kb == 0, kb == 2 * j + 1)
                mm.then_inc(pv_mm, 1)

            def square_sum(h, j):
                n = NPAIR * h + j
                pe.wait_ge(osq_ready, n + 1)
                nc.tensor.matmul(PS[:, 6, 2 * P:4 * P], ones[:, :], o_sq[:, :], start=True, stop=True).then_inc(ss_mm, 1)

            pe.wait_ge(ones_set, 1)
            for h in range(H):
                qk_group(h, 0)
                if h:
                    for g in T_OF_STEP[8]:
                        transposes(h - 1, g)
                    values(h - 1, 2)
                else:
                    y_group(0)
                qk_group(h, 1)
                if h:
                    for g in T_OF_STEP[9]:
                        transposes(h - 1, g)
                    square_sum(h - 1, 2)
                else:
                    y_group(1)
                for s in range(NT):
                    scores(h, s)
                    for g in T_OF_STEP.get(s, []):
                        if g[0] == "T":
                            transposes(h, g)
                    if s == 0:
                        v_part(h, 0, 0, KD)
                        if h:
                            values(h - 1, 3)
                        else:
                            y_group(2)
                    if s == 1:
                        qk_group(h, 2)
                        if h:
                            square_sum(h - 1, 3)
                        else:
                            y_group(3)
                    if s == 2:
                        qk_group(h, 3)
                    if s in (4, 6):
                        values(h, (s - 4) // 2)
                    if 3 <= s <= 6:
                        v_part(h, 1, 2 * (s - 3), 2 * (s - 2))
                    if s in (5, 7):
                        square_sum(h, (s - 5) // 2)
                    for g in T_OF_STEP.get(s, []):
                        if g[0] == "V":
                            transposes(h, g)

            def out_project(p, n0, n1):
                for n in range(n0, n1):
                    e = WO_ORDER[n]
                    if p == 0:
                        pe.wait_ge(wo_lo, n + 1)
                    es = slice(e * P, (e + 1) * P)
                    for i in range(2):
                        c = (2 * p + i) % 4
                        for half in range(2):
                            cols = slice(half * BANK, (half + 1) * BANK)
                            mm = three(bank(4 * (p % 2) + 2 * i + half), w_hi[:, c, es], w_lo[:, c, es],
                                       wout_hi[:, e, cols], wout_lo[:, e, cols], n == 0, n == KD - 1)
                            if n == KD - 1:
                                mm.then_inc(o_mm, 1)

            def x2_tiles(p):
                for t in (2 * p, 2 * p + 1):
                    pe.wait_ge(xn2_ready, t + 1)
                    for j in range(2):
                        b = 4 * (p % 2) + 2 * (t % 2) + j
                        for k in range(4):
                            kk = 4 * j + k
                            tr = nc.tensor.transpose(bank(b)[:, k * P:(k + 1) * P], xn2[:, t % 2, kk * P:(kk + 1) * P],
                                                     ident[:, :])
                        tr.then_inc(tr2, 1)

            h = H - 1
            pe.wait_ge(s_read, 2 * NT * H)
            pe.wait_ge(mx_lo, 2)
            for g in T_OF_STEP[8]:
                transposes(h, g)
            values(h, 2)
            out_project(0, 0, 2)
            for g in T_OF_STEP[9]:
                transposes(h, g)
            square_sum(h, 2)
            out_project(0, 2, 4)
            values(h, 3)
            out_project(0, 4, 6)
            square_sum(h, 3)
            out_project(0, 6, 8)
            for p in range(1, NPAIR):
                pe.wait_ge(mx_lo, 2 * p + 2)
                if p == 1:
                    pe.wait_ge(t_lo, H * T_PER_HEAD)
                    pe.wait_ge(mix_ready, H * NPAIR)
                else:
                    pe.wait_ge(tr2_lo, 4 * (p - 1))
                out_project(p, 0, 4)
                x2_tiles(p - 1)
                out_project(p, 4, 8)

            def gate_up(s, c, half):
                n = 2 * c + half
                if not (isinstance(s, int) and s == 0 and n < 2):
                    pe.wait_ge(gated_ready, s * 4 + (n - 1))
                for kind in range(2):
                    slot = 2 * c + kind
                    if half == 0:
                        pe.wait_ge(fw_lo, s * 4 + (slot + 1))
                    cols = slice(half * HALF, (half + 1) * HALF)
                    for k in range(KD):
                        ws = slice(k * P, (k + 1) * P)
                        mm = three(bank(2 * half + kind), w_hi[:, slot, ws], w_lo[:, slot, ws],
                                   h2T_hi[:, k, cols], h2T_lo[:, k, cols], k == 0, k == KD - 1)
                    mm.then_inc(gu_mm, 1)

            def ff_gate(s):
                for c in range(2):
                    for half in range(2):
                        gate_up(s, c, half)

            def ff_down(s, slot):
                pe.wait_ge(act_ready, s * 4 + 4)
                pe.wait_ge(fd_lo, s + 1)
                for t in range(NT):
                    ts = slice(t * P, (t + 1) * P)
                    for half in range(2):
                        n = 2 * t + half
                        pe.wait_ge(d_free, s * 16 + (n + 1))
                        cols = slice(half * BANK, (half + 1) * BANK)
                        for c in range(2):
                            mm = three(bank(4 + n % 4), act_hi[:, slot, c, ts], act_lo[:, slot, c, ts],
                                       dn_hi[:, c, cols], dn_lo[:, c, cols], c == 0, c == 1)
                        mm.then_inc(d_mm, 1)

            pe.wait_ge(tr2_lo, 4 * (NPAIR - 1))
            gate_up(0, 0, 0)
            x2_tiles(NPAIR - 1)
            pe.wait_ge(d_free, 4)
            gate_up(0, 0, 1)
            gate_up(0, 1, 0)
            gate_up(0, 1, 1)
            with nc.Fori(0, STEPS // 2 - 1, engines=[ENG.PE]) as i:
                ff_gate(i * 2 + 1)
                ff_down(i * 2, 0)
                ff_gate(i * 2 + 2)
                ff_down(i * 2 + 1, 1)
            ff_gate(STEPS - 2)
            ff_down(STEPS - 3, 0)
            ff_gate(STEPS - 1)
            ff_down(STEPS - 2, 1)
            ff_down(STEPS - 1, 0)


_INS = ["x", "norm1_g", "w_in", "lam_qk", "subln_g", "pool_w", "pool_scale", "w_out",
        "norm2_g", "w_gate", "w_up", "w_down", "final_g"]


def kernel(**inputs):
    import numpy as _np
    import concourse.bacc as _bacc
    from concourse import mybir as _mybir
    from concourse.bass_utils import run_bass_kernel_spmd as _run

    nc = _bacc.Bacc("TRN2", target_bir_lowering=False, num_devices=1, dynamic_dma_scratch_size=DMA_SCRATCH)
    arrays, args = {}, []
    for name in _INS:
        a = _np.ascontiguousarray(inputs[name])
        arrays[f"in_{name}_dram"] = a
        args.append(nc.dram_tensor(f"in_{name}_dram", a.shape, _mybir.dt.from_np(a.dtype), kind="ExternalInput").ap())
    shape = _np.shape(inputs["x"])
    args.append(nc.dram_tensor("out_0_dram", shape, _mybir.dt.float32, kind="ExternalOutput").ap())
    hybrid_block(nc, *args)
    r = _run(nc, [arrays], core_ids=[0])
    return r.results[0]["out_0_dram"]
```

```python
import math
from contextlib import ExitStack

import concourse.bass as bass
from concourse import mybir

F32 = mybir.dt.float32
F32R = mybir.dt.float32r
ALU = mybir.AluOpType
ACT = mybir.ActivationFunctionType
ENG = mybir.EngineType

P = 128
BANK = 512
POOL_WINDOWS = (2, 4, 8, 16)
NORM_EPS = 1e-5
LAMBDA_INIT = 0.8 - 0.6 * math.exp(-0.3 * 0)
MASKED = -1.0e30
LOWEST = -3.0e38
DMA_SCRATCH = 1024
KIB = 1024


def hybrid_block(nc, x, norm1_g, w_in, lam_qk, subln_g, pool_w, pool_scale, w_out,
                 norm2_g, w_gate, w_up, w_down, final_g, out):
    _, SEQ, D = x.shape
    HD = lam_qk.shape[2]
    VD = subln_g.shape[1]
    POOL = pool_scale.shape[1]
    G = POOL // P
    ATTN = D - POOL
    H = ATTN // VD
    FF = w_gate.shape[2]
    NT = SEQ // P
    KD = D // P
    NF = FF // P
    STEPS = NF // 2
    HALF = SEQ // 2
    assert VD == P == 2 * HD and HALF == BANK and D == 2 * BANK and NT == KD == 8 and H == G == 4
    assert NF % 2 == 0 and STEPS % 2 == 1
    SCALE = HD ** -0.5

    with ExitStack() as ctx:
        def sem(name):
            return ctx.enter_context(nc.semaphore(name))

        R0 = 2 * KIB
        R1 = R0 + 64 * KIB
        R2 = R1 + 32 * KIB
        R3 = R2 + 64 * KIB
        RC = R3 + 48 * KIB

        def at(name, offset, shape, dt=F32):
            return nc.alloc_sbuf_tensor_at(name, [P, *shape], dt, offset=offset)

        hT_hi = at("hT_hi", R0, [KD, SEQ], F32R)
        hT_lo = at("hT_lo", R0 + 32 * KIB, [KD, SEQ], F32R)
        wout_hi = at("wout_hi", R0, [KD, D], F32R)
        wout_lo = at("wout_lo", R0 + 32 * KIB, [KD, D], F32R)
        act_hi = at("act_hi", R0, [2, 2, SEQ], F32R)
        act_lo = at("act_lo", R0 + 16 * KIB, [2, 2, SEQ], F32R)
        dn_hi = at("dn_hi", R0 + 32 * KIB, [2, D], F32R)
        dn_lo = at("dn_lo", R0 + 40 * KIB, [2, D], F32R)
        dn_raw = at("dn_raw", R0 + 48 * KIB, [2, D])
        silu_g = at("silu_g", R0 + 56 * KIB, [2, BANK])
        gated = at("gated", R0 + 60 * KIB, [2, BANK])

        x_in = at("x_in", R1, [NT, D])
        mixT = at("mixT", R1, [KD, SEQ])
        h2T_hi = at("h2T_hi", R1, [KD, SEQ], F32R)

        q_hi = at("q_hi", R2, [SEQ], F32R)
        q_lo = at("q_lo", R2 + 4 * KIB, [SEQ], F32R)
        k_hi = at("k_hi", R2 + 8 * KIB, [SEQ], F32R)
        k_lo = at("k_lo", R2 + 12 * KIB, [SEQ], F32R)
        v_hi = at("v_hi", R2 + 16 * KIB, [NT, P], F32R)
        v_lo = at("v_lo", R2 + 20 * KIB, [NT, P], F32R)
        vT = at("vT", R2 + 24 * KIB, [SEQ])
        prob = at("prob", R2 + 28 * KIB, [2, 2, SEQ])
        attT_hi = at("attT_hi", R2 + 44 * KIB, [NT, 2 * P], F32R)
        attT_lo = at("attT_lo", R2 + 52 * KIB, [NT, 2 * P], F32R)
        o_sq = at("o_sq", R2 + 60 * KIB, [2 * P])
        o_rstd = at("o_rstd", R2 + 61 * KIB, [2 * P])
        junk = at("junk", R2 + 24 * KIB, [D])
        xn = at("xn", R2 + 28 * KIB, [2, D])
        PAD = max(POOL_WINDOWS)
        win = [at(f"win{i}", R2 + (28 + 5 * i) * KIB, [PAD + SEQ]) for i in range(2)]
        resid = [at("resid0", R2 + 38 * KIB, [SEQ]), at("resid1", R2 + 12 * KIB, [SEQ])]
        pw_raw = at("pw_raw", R2 + 16 * KIB, [G, P])
        pw_hi = at("pw_hi", R2 + 18 * KIB, [G, P], F32R)
        pw_lo = at("pw_lo", R2 + 20 * KIB, [G, P], F32R)
        res_hi = at("res_hi", R2 + 44 * KIB, [2, SEQ], F32R)
        res_lo = at("res_lo", R2 + 52 * KIB, [2, SEQ], F32R)
        x2 = at("x2", R2, [NT, D])
        h2T_lo = at("h2T_lo", R2 + 32 * KIB, [KD, SEQ], F32R)

        w_raw = at("w_raw", R3, [4, D])
        w_hi = at("w_hi", R3 + 16 * KIB, [4, D], F32R)
        w_lo = at("w_lo", R3 + 32 * KIB, [4, D], F32R)

        g1_row = at("g1_row", RC, [D])
        mask = at("mask", RC + 4 * KIB, [SEQ])
        xn2 = at("xn2", RC, [2, D])
        g2_row = at("g2_row", RC + 8 * KIB, [D])
        gf_row = at("gf_row", RC + 8 * KIB, [D])
        ident = at("ident", RC + 12 * KIB, [P])
        ones = at("ones", RC + 12 * KIB + 512, [P])
        lam_in = at("lam_in", R2, [4, HD])
        lam_pr = at("lam_pr", R2 + KIB, [2, HD])
        small = RC + 13 * KIB - 1536
        lam_sum = at("lam_sum", small + 1536, [2])
        lam_exp = at("lam_exp", small + 1568, [2])
        neg_lam = at("neg_lam", small + 1600, [2])
        subln_c = at("subln_c", small + 1632, [2])
        pscale_c = at("pscale_c", small + 1664, [G])
        inv_cnt = at("inv_cnt", small + 1696, [PAD])
        fix = at("fix", small + 1760, [PAD])
        eps_c = at("eps_c", small + 1824, [1])
        mhalf = at("mhalf", small + 1856, [NT])
        ss1 = at("ss1", small + 1888, [NT])
        rs1 = at("rs1", small + 1920, [NT])
        ss2 = at("ss2", small + 1952, [NT])
        rs2 = at("rs2", small + 1984, [NT])
        ss3 = at("ss3", small + 2016, [2 * NT])
        rs3 = at("rs3", small + 2080, [NT])
        smax = at("smax", small + 2112, [2, 2])
        nbias = at("nbias", small + 2144, [2, 2])
        lsum = at("lsum", small + 2176, [2, 2])
        rsum = at("rsum", small + 2208, [2, 2])
        ms = at("ms", small + 2240, [NT])

        PS = ctx.enter_context(nc.psum_tensor("PS", [P, 8, BANK], F32))

        def bank(b):
            return PS[:, b, :]

        def blocks(b, n=4):
            return PS[:, b, 0:n * P].rearrange("p (n c) -> p n c", c=P)

        x_in_here = [sem(f"x_in_here{t}") for t in range(NT)]
        x2_here = [sem(f"x2_here{i}") for i in range(NT // 2)]
        small_here, g1_here, g2_here, gf_here = sem("small_here"), sem("g1_here"), sem("g2_here"), sem("gf_here")
        raw_here = [sem(f"raw_here{i}") for i in range(4)]
        pw_here = sem("pw_here")
        dn_here = sem("dn_here")
        ident_set, mhalf_set, ones_set, eps_set, pads_set, mask_set, cnt_set = (
            sem("ident_set"), sem("mhalf_set"), sem("ones_set"), sem("eps_set"), sem("pads_set"),
            sem("mask_set"), sem("cnt_set"))
        dvec = sem("dvec")
        lam_ready, lam_a = sem("lam_ready"), sem("lam_a")
        sq1, pow1 = sem("sq1"), sem("pow1")
        poolc = sem("poolc")
        xn_ready = sem("xn_ready")
        tr1, tr1_hi, tr1_lo = sem("tr1"), sem("tr1_hi"), sem("tr1_lo")
        whi, wlo = sem("whi"), sem("wlo")
        u_mm, u_raw = sem("u_mm"), sem("u_raw")
        res_ready, res_hi_ready, res_lo_ready = sem("res_ready"), sem("res_hi_ready"), sem("res_lo_ready")
        y_mm, y_out = sem("y_mm"), sem("y_out")
        qk_mm, qk_hi, qk_lo = sem("qk_mm"), sem("qk_hi"), sem("qk_lo")
        v_mm, v_raw = sem("v_mm"), sem("v_raw")
        s_mm, s_read, nb_ready, exp_done, att_ready = (
            sem("s_mm"), sem("s_read"), sem("nb_ready"), sem("exp_done"), sem("att_ready"))
        t_mm, t_hi, t_lo = sem("t_mm"), sem("t_hi"), sem("t_lo")
        pv_mm, osq_ready, ss_mm, ln_done, rstd_ready, mix_ready = (
            sem("pv_mm"), sem("osq_ready"), sem("ss_mm"), sem("ln_done"), sem("rstd_ready"), sem("mix_ready"))
        mx_hi, mx_lo = sem("mx_hi"), sem("mx_lo")
        wo_hi, wo_lo = sem("wo_hi"), sem("wo_lo")
        o_mm, x2_add, sq2, pow2, xn2_ready = sem("o_mm"), sem("x2_add"), sem("sq2"), sem("pow2"), sem("xn2_ready")
        tr2, tr2_hi, tr2_lo = sem("tr2"), sem("tr2_hi"), sem("tr2_lo")
        fw_hi, fw_lo, fd_hi, fd_lo = sem("fw_hi"), sem("fw_lo"), sem("fd_hi"), sem("fd_lo")
        gu_mm, silu_done, gated_ready, act_hi_ready, act_ready = (
            sem("gu_mm"), sem("silu_done"), sem("gated_ready"), sem("act_hi_ready"), sem("act_ready"))
        d_mm = sem("d_mm")
        d_free = sem("d_free")
        sq3, pow3, y_ready, out_done = sem("sq3"), sem("pow3"), sem("y_ready"), sem("out_done")

        def blk_u(g):
            return g + 1
        BLK_PW = G + 1

        def blk_qkv(h, c):
            return G + 1 + 3 * h + c + 1
        BLKS = G + 1 + 3 * H

        def t_groups(qt):
            n = qt + 1
            return [("T", qt, k0, min(4, n - k0)) for k0 in range(0, n, 4)]
        T_OF_STEP = {2: t_groups(0), 3: t_groups(1) + [("V", 0, 0, 4)], 4: t_groups(2), 5: t_groups(3) + [("V", 1, 4, 4)],
                     6: t_groups(4), 7: t_groups(5), 8: t_groups(6), 9: t_groups(7)}
        T_ORDER = [g for s in range(2, 10) for g in T_OF_STEP[s]]
        T_PER_HEAD = len(T_ORDER)
        assert T_PER_HEAD % 2 == 0

        def t_index(h, group):
            return h * T_PER_HEAD + T_ORDER.index(group)

        def last_group(h, kind, n):
            return max(t_index(h, g) for g in T_ORDER if g[0] == kind and g[1] == n) + 1

        def tr1_bank(t, j):
            return 4 + 2 * (t % 2) + j

        QK_BANK = (7, 2, 3, 7)
        V_BANK = (7, 1)

        def y_bank(g, half):
            return ((6, 1), (4, 5))[g % 2][half]

        NPAIR = NT // 2
        WO_ORDER = list(range(H, KD)) + list(range(H))

        def wo_slot(n):
            return (n + 3) % 4

        block = ctx.enter_context(nc.Block())

        @block.sync
        def _(sp):
            xt = x[0].rearrange("(t p) d -> p t d", p=P)
            w_in_v = w_in[0].rearrange("(k p) n -> p k n", p=P)
            w_out_v = w_out[0].rearrange("(k p) n -> p k n", p=P)
            gate_v = w_gate[0].rearrange("(k p) n -> p k n", p=P)
            up_v = w_up[0].rearrange("(k p) n -> p k n", p=P)
            down_v = w_down[0].rearrange("(f p) n -> p f n", p=P)
            slot = [w_raw[:, c, :].rearrange("p (k n) -> p k n", k=KD) for c in range(4)]

            def load_x(t):
                sp.dma_start(x_in[:, t, :], xt[:, t, :]).then_inc(x_in_here[t], 16)

            def load_in(c, col):
                sp.dma_start(slot[c], w_in_v[:, :, col:col + P]).then_inc(raw_here[c], 16)

            load_x(0)
            sp.dma_start(g1_row[:, :], norm1_g[0:1, :].to_broadcast([P, D])).then_inc(g1_here, 16)
            load_x(1)
            load_x(2)
            load_in(0, 3 * ATTN)
            load_x(3)
            load_in(1, 3 * ATTN + P)
            load_x(4)
            load_x(5)
            load_in(2, 3 * ATTN + 2 * P)
            load_x(6)
            load_in(3, 3 * ATTN + 3 * P)
            load_x(7)
            sp.dma_start(pw_raw[:, :, :], pool_w[0].rearrange("g c n -> c g n")).then_inc(pw_here, 16)
            sp.dma_start(lam_in[:, :, :], lam_qk[0:1, :, :].to_broadcast([P, 4, HD])).then_inc(small_here, 16)
            sp.dma_start(subln_c[:, 0:1], subln_g.rearrange("a (d b) -> (a d) b", b=1)).then_inc(small_here, 16)
            for g in range(G):
                sp.dma_start(pscale_c[:, g:g + 1], pool_scale[0].rearrange("(g p b) -> g p b", p=P, b=1)[g])\
                  .then_inc(small_here, 16)
            sp.dma_start(g2_row[:, :], norm2_g[0:1, :].to_broadcast([P, D])).then_inc(g2_here, 16)
            for h in range(H):
                for c in range(3):
                    sp.wait_ge(wlo, blk_u(c) if h == 0 else blk_qkv(h - 1, c))
                    load_in(c, c * ATTN + h * P)
            for n, e in enumerate(WO_ORDER):
                if n == 0:
                    sp.wait_ge(wlo, blk_u(3))
                elif n < 4:
                    sp.wait_ge(wlo, blk_qkv(H - 1, wo_slot(n)))
                else:
                    sp.wait_ge(wo_lo, n - 3)
                sp.dma_start(w_raw[:, wo_slot(n), :], w_out_v[:, e, :]).then_inc(raw_here[wo_slot(n)], 16)
            sp.wait_ge(s_mm, H * NT)
            for i in range(NT // 2):
                if i == 2:
                    sp.wait_ge(pv_mm, H * NPAIR)
                    sp.wait_ge(t_mm, H * T_PER_HEAD)
                sp.dma_start(x2[:, 2 * i:2 * i + 2, :], xt[:, 2 * i:2 * i + 2, :]).then_inc(x2_here[i], 16)

            def load_gu(s, c, kind):
                src = (gate_v, up_v)[kind]
                cols = bass.ds(s * 2 * P + c * P, P) if not isinstance(s, int) else slice(s * 2 * P + c * P, s * 2 * P + c * P + P)
                sp.dma_start(slot[2 * c + kind], src[:, :, cols]).then_inc(raw_here[2 * c + kind], 16)

            for c in range(4):
                n = max(m for m in range(KD) if wo_slot(m) == c)
                sp.wait_ge(wo_lo, n + 1)
                load_gu(0, c // 2, c % 2)
            sp.wait_ge(o_mm, 4 * NPAIR)
            sp.dma_start(dn_raw[:, :, :], down_v[:, 0:2, :]).then_inc(dn_here, 16)
            sp.wait_ge(xn2_ready, NT)
            sp.dma_start(gf_row[:, :], final_g.rearrange("(a d) -> a d", a=1).to_broadcast([P, D])).then_inc(gf_here, 16)
            with nc.Fori(1, STEPS, engines=[ENG.SP]) as s:
                for c in range(4):
                    sp.wait_ge(fw_lo, s * 4 + (c - 3))
                    load_gu(s, c // 2, c % 2)
                sp.wait_ge(fd_lo, s)
                sp.dma_start(dn_raw[:, :, :], down_v[:, bass.ds(s * 2, 2), :]).then_inc(dn_here, 16)
            for t in range(NT):
                sp.wait_ge(y_ready, t + 1)
                sp.dma_start(out[0, t * P:(t + 1) * P, :], x2[:, t, :]).then_inc(out_done, 16)
            sp.wait_ge(out_done, 16 * NT)

        @block.gpsimd
        def _(gp):
            chain = [0]

            def link(ins):
                chain[0] += 1
                ins.then_inc(poolc, 1)
                gp.wait_ge(poolc, chain[0])

            link(nc.gpsimd.memset(ident[:, :], 0.0))
            nc.gpsimd.affine_select(out=ident[:, :], in_=ident[:, :], compare_op=ALU.not_equal, fill=1.0,
                                    base=0, pattern=[[-1, P]], channel_multiplier=1).then_inc(ident_set, 1)
            nc.gpsimd.memset(mhalf[:, :], -0.5).then_inc(mhalf_set, 1)
            gp.wait_ge(mhalf_set, 1)

            nc.gpsimd.memset(ones[:, :], 1.0).then_inc(ones_set, 1)
            nc.gpsimd.memset(eps_c[:, :], NORM_EPS).then_inc(eps_set, 1)
            for j in range(PAD):
                nc.gpsimd.memset(inv_cnt[:, j:j + 1], 1.0 / (j + 1)).then_inc(cnt_set, 1)
            link(nc.gpsimd.memset(mask[:, :], 0.0))
            nc.gpsimd.affine_select(out=mask[:, SEQ - P:SEQ], in_=mask[:, SEQ - P:SEQ], compare_op=ALU.is_ge,
                                    fill=MASKED, base=0, pattern=[[-1, P]], channel_multiplier=1).then_inc(mask_set, 1)

            def low(c, n):
                gp.wait_ge(whi, n)
                nc.gpsimd.tensor_tensor(w_lo[:, c, :], w_raw[:, c, :], w_hi[:, c, :].bitcast(F32),
                                        ALU.subtract).then_inc(wlo, 1)

            def pow_x(t):
                gp.wait_ge(sq1, t + 1)
                link(nc.gpsimd.tensor_scalar(ms[:, t:t + 1], ss1[:, t:t + 1], 1.0 / D, NORM_EPS, ALU.mult, ALU.add))
                nc.gpsimd.tensor_tensor(rs1[:, t:t + 1], ms[:, t:t + 1], mhalf[:, 0:1], ALU.pow).then_inc(pow1, 1)

            for t in range(4):
                pow_x(t)
            low(0, blk_u(0))
            low(1, blk_u(1))
            pow_x(4)
            pow_x(5)
            low(2, blk_u(2))
            pow_x(6)
            pow_x(7)
            low(3, blk_u(3))
            gp.wait_ge(whi, BLK_PW)
            nc.gpsimd.tensor_tensor(pw_lo[:, :, :], pw_raw[:, :, :], pw_hi[:, :, :].bitcast(F32),
                                    ALU.subtract).then_inc(wlo, 1)
            gp.wait_ge(tr1, 2 * NT)
            for i in range(2):
                nc.gpsimd.memset(win[i][:, 0:PAD], 0.0).then_inc(pads_set, 1)
            for h in range(H):
                for c in range(3):
                    low(c, blk_qkv(h, c))
            for n, e in enumerate(WO_ORDER):
                gp.wait_ge(wo_hi, n + 1)
                nc.gpsimd.tensor_tensor(wout_lo[:, e, :], w_raw[:, wo_slot(n), :], wout_hi[:, e, :].bitcast(F32),
                                        ALU.subtract).then_inc(wo_lo, 1)

            def pow_x2(t):
                gp.wait_ge(sq2, t + 1)
                link(nc.gpsimd.tensor_scalar(ms[:, t:t + 1], ss2[:, t:t + 1], 1.0 / D, NORM_EPS, ALU.mult, ALU.add))
                nc.gpsimd.tensor_tensor(rs2[:, t:t + 1], ms[:, t:t + 1], mhalf[:, 0:1], ALU.pow).then_inc(pow2, 1)

            def low_gu(s, c):
                gp.wait_ge(fw_hi, s * 4 + c + 1)
                nc.gpsimd.tensor_tensor(w_lo[:, c, :], w_raw[:, c, :], w_hi[:, c, :].bitcast(F32),
                                        ALU.subtract).then_inc(fw_lo, 1)

            def low_dn(s):
                gp.wait_ge(fd_hi, s + 1)
                nc.gpsimd.tensor_tensor(dn_lo[:, :, :], dn_raw[:, :, :], dn_hi[:, :, :].bitcast(F32),
                                        ALU.subtract).then_inc(fd_lo, 1)

            for t in range(NT - 2):
                pow_x2(t)
            low_gu(0, 0)
            low_gu(0, 1)
            pow_x2(NT - 2)
            pow_x2(NT - 1)
            low_gu(0, 2)
            low_gu(0, 3)
            with nc.Fori(1, STEPS, engines=[ENG.Pool]) as s:
                for c in range(4):
                    low_gu(s, c)
                low_dn(s - 1)
            low_dn(STEPS - 1)
            for t in range(NT):
                gp.wait_ge(sq3, 2 * t + 2)
                link(nc.gpsimd.tensor_tensor(ms[:, t:t + 1], ss3[:, 2 * t:2 * t + 1], ss3[:, 2 * t + 1:2 * t + 2], ALU.add))
                link(nc.gpsimd.tensor_scalar(ms[:, t:t + 1], ms[:, t:t + 1], 1.0 / D, NORM_EPS, ALU.mult, ALU.add))
                nc.gpsimd.tensor_tensor(rs3[:, t:t + 1], ms[:, t:t + 1], mhalf[:, 0:1], ALU.pow).then_inc(pow3, 1)

        @block.scalar
        def _(act):
            nc.scalar.preload_act_table_set("natural_log_exp_and_others")

            def split_hi(c, count):
                act.wait_ge(raw_here[c], 16 * count)
                nc.scalar.copy(w_hi[:, c, :], w_raw[:, c, :]).then_inc(whi, 1)

            def hi_x(t):
                for j in range(2):
                    act.wait_ge(tr1, 2 * t + j + 1)
                    nc.scalar.copy(hT_hi[:, 4 * j:4 * j + 4, t * P:(t + 1) * P],
                                   blocks(tr1_bank(t, j))).then_inc(tr1_hi, 1)

            def square_x(t):
                act.wait_ge(x_in_here[t], 16)
                if t:
                    act.wait_ge(sq1, t)
                nc.scalar.activation(junk[:, :], x_in[:, t, :], ACT.Square, accum_out=ss1[:, t:t + 1]).then_inc(sq1, 1)

            square_x(0)
            square_x(1)
            square_x(2)
            hi_x(0)
            square_x(3)
            hi_x(1)
            split_hi(0, 1)
            hi_x(2)
            split_hi(1, 1)
            hi_x(3)
            square_x(4)
            square_x(5)
            split_hi(2, 1)
            hi_x(4)
            square_x(6)
            square_x(7)
            split_hi(3, 1)
            hi_x(5)
            act.wait_ge(pw_here, 16)
            nc.scalar.copy(pw_hi[:, :, :], pw_raw[:, :, :]).then_inc(whi, 1)
            hi_x(6)
            hi_x(7)

            def u_copy(n):
                half, g = divmod(n, G)
                act.wait_ge(u_mm, n + 1)
                nc.scalar.copy(mixT[:, H + g, half * HALF:(half + 1) * HALF], bank(n % 4)).then_inc(u_raw, 1)

            def res_high(g):
                act.wait_ge(res_ready, g + 1)
                if g >= 2:
                    act.wait_ge(y_mm, 2 * (g - 1))
                nc.scalar.copy(res_hi[:, g % 2, :], resid[g % 2][:, :]).then_inc(res_hi_ready, 1)

            def y_copy(g):
                for half in range(2):
                    act.wait_ge(y_mm, 2 * g + half + 1)
                    nc.scalar.activation(mixT[:, H + g, half * HALF:(half + 1) * HALF], bank(y_bank(g, half)),
                                         ACT.Copy, scale=pscale_c[:, g:g + 1]).then_inc(y_out, 1)

            act.wait_ge(xn_ready, NT)
            for n in range(G):
                u_copy(n)
            u_copy(G)
            split_hi(0, 2)
            u_copy(G + 1)
            split_hi(1, 2)
            res_high(0)
            u_copy(G + 2)
            split_hi(2, 2)
            res_high(1)
            u_copy(G + 3)
            act.wait_ge(lam_ready, 1)
            nc.scalar.activation(lam_exp[:, :], lam_sum[:, :], ACT.Exp).then_inc(lam_a, 1)
            y_copy(0)
            y_copy(1)

            def qk_high(h, n):
                act.wait_ge(qk_mm, 4 * h + n + 1)
                dst = (q_hi, k_hi)[n % 2]
                nc.scalar.copy(dst[:, (n // 2) * HALF:(n // 2 + 1) * HALF], bank(QK_BANK[n])).then_inc(qk_hi, 1)

            def v_copy(h, half):
                act.wait_ge(v_mm, 2 * h + half + 1)
                if h:
                    act.wait_ge(t_mm, last_group(h - 1, "V", half))
                nc.scalar.copy(vT[:, half * HALF:(half + 1) * HALF], bank(V_BANK[half])).then_inc(v_raw, 1)

            def t_high(h, group):
                kind, n, k0, nb = group
                i = t_index(h, group)
                act.wait_ge(t_mm, i + 1)
                if kind == "V":
                    if h:
                        act.wait_ge(pv_mm, NPAIR * h)
                    dst = v_hi[:, k0:k0 + nb, :]
                else:
                    done = NPAIR * h + n // 2
                    if done:
                        act.wait_ge(pv_mm, done)
                    dst = attT_hi[:, k0:k0 + nb, (n % 2) * P:(n % 2 + 1) * P]
                nc.scalar.copy(dst, blocks(4 + i % 2, nb)).then_inc(t_hi, 1)

            def exps(h, s):
                n = NT * h + s
                L = (s + 1) * P
                act.wait_ge(nb_ready, n + 1)
                for r in range(2):
                    nc.scalar.activation(prob[:, s % 2, r, 0:L], prob[:, s % 2, r, 0:L], ACT.Exp,
                                         bias=nbias[:, s % 2, r:r + 1], scale=SCALE,
                                         accum_out=lsum[:, s % 2, r:r + 1]).then_inc(exp_done, 1)

            def o_square(h, j):
                n = NPAIR * h + j
                act.wait_ge(pv_mm, n + 1)
                if n:
                    act.wait_ge(ss_mm, n)
                nc.scalar.activation(o_sq[:, :], PS[:, 6, 0:2 * P], ACT.Square).then_inc(osq_ready, 1)

            def o_rsqrt(h, j):
                n = NPAIR * h + j
                act.wait_ge(ss_mm, n + 1)
                if n:
                    act.wait_ge(mix_ready, n)
                nc.scalar.activation(o_rstd[:, :], PS[:, 6, 2 * P:4 * P], ACT.Ln, bias=eps_c[:, 0:1],
                                     scale=1.0 / VD).then_inc(ln_done, 1)
                act.wait_ge(ln_done, n + 1)
                nc.scalar.activation(o_rstd[:, :], o_rstd[:, :], ACT.Exp, scale=-0.5).then_inc(rstd_ready, 1)

            def wout_high(n):
                e, c = WO_ORDER[n], wo_slot(n)
                count = (1 if c == 3 else 1 + H) + 1 + (n >= 4)
                if n == 0:
                    act.wait_ge(v_mm, 2 * H)
                act.wait_ge(raw_here[c], 16 * count)
                nc.scalar.copy(wout_hi[:, e, :], w_raw[:, c, :]).then_inc(wo_hi, 1)

            def mix_high(t):
                if t == 0:
                    act.wait_ge(qk_mm, 4 * H)
                if t == 2:
                    act.wait_ge(v_mm, 2 * H)
                act.wait_ge(mix_ready, NPAIR * (H - 1) + t // 2 + 1)
                if t >= 4:
                    act.wait_ge(o_mm, 4 * (t // 2 - 1))
                nc.scalar.copy(w_hi[:, t % 4, :].rearrange("p (e n) -> p e n", e=KD),
                               mixT[:, :, t * P:(t + 1) * P]).then_inc(mx_hi, 1)

            act.wait_ge(eps_set, 1)
            qk_high(0, 0)
            res_high(2)
            res_high(3)
            y_copy(2)
            for h in range(H):
                if h:
                    for g in T_OF_STEP[8]:
                        t_high(h - 1, g)
                    o_square(h - 1, 2)
                qk_high(h, 1)
                if h:
                    for g in T_OF_STEP[9]:
                        t_high(h - 1, g)
                    o_rsqrt(h - 1, 2)
                else:
                    y_copy(3)
                for s in range(NT):
                    for g in T_OF_STEP.get(s, []):
                        if g[0] == "T":
                            t_high(h, g)
                    exps(h, s)
                    if s == 0:
                        v_copy(h, 0)
                        if h:
                            o_square(h - 1, 3)
                    if s == 1:
                        qk_high(h, 2)
                        if h:
                            o_rsqrt(h - 1, 3)
                    if s == 2:
                        qk_high(h, 3)
                    if s == 3:
                        v_copy(h, 1)
                    if s in (4, 6):
                        o_square(h, (s - 4) // 2)
                    if s in (5, 7):
                        o_rsqrt(h, (s - 5) // 2)
                    for g in T_OF_STEP.get(s, []):
                        if g[0] == "V":
                            t_high(h, g)
                    if h + 1 < H:
                        if s == 2:
                            act.wait_ge(qk_mm, 4 * h + 3)
                            split_hi(0, 3 + h)
                        if s == 3:
                            act.wait_ge(qk_mm, 4 * h + 4)
                            split_hi(1, 3 + h)
                        if s == 4:
                            act.wait_ge(v_mm, 2 * h + 2)
                            split_hi(2, 3 + h)
                        if s == 7:
                            qk_high(h + 1, 0)
                    elif s >= 4:
                        wout_high(s - 4)
                        if s >= 6:
                            mix_high(s - 6)
            h = H - 1
            for g in T_OF_STEP[8]:
                t_high(h, g)
            o_square(h, 2)
            wout_high(4)
            for g in T_OF_STEP[9]:
                t_high(h, g)
            o_rsqrt(h, 2)
            wout_high(5)
            o_square(h, 3)
            wout_high(6)
            o_rsqrt(h, 3)
            wout_high(7)
            mix_high(2)
            mix_high(3)

            def square_x2(t):
                act.wait_ge(x2_add, 2 * t + 2)
                if t >= 2:
                    act.wait_ge(tr2, 2 * (t - 1))
                nc.scalar.activation(xn2[:, t % 2, :], x2[:, t, :], ACT.Square, accum_out=ss2[:, t:t + 1]).then_inc(sq2, 1)

            def hi_x2(t):
                for j in range(2):
                    act.wait_ge(tr2, 2 * t + j + 1)
                    act.wait_ge(mx_lo, t + 1)
                    nc.scalar.copy(h2T_hi[:, 4 * j:4 * j + 4, t * P:(t + 1) * P],
                                   blocks(4 * ((t // 2) % 2) + 2 * (t % 2) + j)).then_inc(tr2_hi, 1)

            def gu_high(s, c):
                act.wait_ge(raw_here[c], (s + FIRST_GU[c]) * 16)
                nc.scalar.copy(w_hi[:, c, :], w_raw[:, c, :]).then_inc(fw_hi, 1)

            def dn_high(s):
                act.wait_ge(dn_here, s * 16 + 16)
                nc.scalar.copy(dn_hi[:, :, :], dn_raw[:, :, :]).then_inc(fd_hi, 1)

            FIRST_GU = [1 + H + sum(wo_slot(n) == c for n in range(KD)) + 1 for c in range(3)] \
                + [1 + sum(wo_slot(n) == 3 for n in range(KD)) + 1]

            for p in range(NPAIR):
                square_x2(2 * p)
                square_x2(2 * p + 1)
                if p + 2 < NPAIR:
                    mix_high(2 * p + 4)
                    mix_high(2 * p + 5)
                if p == 2:
                    gu_high(0, 0)
                    gu_high(0, 1)
                if p < NPAIR - 1:
                    hi_x2(2 * p)
                    hi_x2(2 * p + 1)

            def gate_up(s, c, half, slot):
                n = 2 * c + half
                act.wait_ge(gu_mm, s * 8 + 2 * n + 1)
                if not (isinstance(s, int) and s == 0 and n < 2):
                    act.wait_ge(gated_ready, s * 4 + n - 1)
                nc.scalar.activation(silu_g[:, n % 2, :], bank(2 * half), ACT.Silu).then_inc(silu_done, 1)
                act.wait_ge(gated_ready, s * 4 + n + 1)
                nc.scalar.copy(act_hi[:, slot, c, half * HALF:(half + 1) * HALF], gated[:, n % 2, :]).then_inc(act_hi_ready, 1)

            def ff_act(s, slot, first=False, last=False):
                for c in range(2):
                    for half in range(2):
                        gate_up(s, c, half, slot)
                        if first and c == 0 and half == 0:
                            hi_x2(NT - 2)
                            hi_x2(NT - 1)
                            gu_high(0, 2)
                            gu_high(0, 3)
                    if not last:
                        act.wait_ge(gu_mm, s * 8 + (4 * c + 4))
                        gu_high(s + 1, 2 * c)
                        gu_high(s + 1, 2 * c + 1)
                if not first:
                    act.wait_ge(d_mm, s * 16)
                dn_high(s)

            act.wait_ge(o_mm, 4 * NPAIR)
            ff_act(0, 0, first=True)
            with nc.Fori(0, STEPS // 2 - 1, engines=[ENG.Activation]) as i:
                ff_act(i * 2 + 1, 1)
                ff_act(i * 2 + 2, 0)
            ff_act(STEPS - 2, 1)
            ff_act(STEPS - 1, 0, last=True)

            for t in range(NT):
                for half in range(2):
                    act.wait_ge(d_free, 4 + 16 * (STEPS - 1) + 2 * t + half + 1)
                    n = 2 * t + half
                    if n >= 2:
                        act.wait_ge(sq3, n - 1)
                    nc.scalar.activation(gated[:, n % 2, :], x2[:, t, half * BANK:(half + 1) * BANK], ACT.Square,
                                         accum_out=ss3[:, n:n + 1]).then_inc(sq3, 1)

        @block.vector
        def _(ve):
            chain = [0]

            def link(ins):
                chain[0] += 1
                ins.then_inc(dvec, 1)
                ve.wait_ge(dvec, chain[0])

            def x_norm(t):
                ve.wait_ge(x_in_here[t], 16)
                ve.wait_ge(pow1, t + 1)
                if t >= 2:
                    ve.wait_ge(tr1, 2 * t - 2)
                nc.vector.scalar_tensor_tensor(out=xn[:, t % 2, :], in0=x_in[:, t, :], scalar=rs1[:, t:t + 1],
                                               in1=g1_row[:, :], op0=ALU.mult, op1=ALU.mult).then_inc(xn_ready, 1)

            def lo_x(t):
                for j in range(2):
                    ve.wait_ge(tr1_hi, 2 * t + j + 1)
                    cols = slice(t * P, (t + 1) * P)
                    nc.vector.tensor_tensor(hT_lo[:, 4 * j:4 * j + 4, cols], blocks(tr1_bank(t, j)),
                                            hT_hi[:, 4 * j:4 * j + 4, cols].bitcast(F32),
                                            ALU.subtract).then_inc(tr1_lo, 1)

            ve.wait_ge(g1_here, 16)
            x_norm(0)
            for t in range(1, NT):
                if t != 4:
                    x_norm(t)
                lo_x(t - 1)
                if t == 4:
                    x_norm(4)
            lo_x(NT - 1)

            ve.wait_ge(small_here, 16 * (2 + G))
            for r in range(2):
                link(nc.vector.tensor_tensor(lam_pr[:, r, :], lam_in[:, 2 * r, :], lam_in[:, 2 * r + 1, :], ALU.mult))
                nc.vector.reduce_sum(lam_sum[:, r:r + 1], lam_pr[:, r, :], mybir.AxisListType.X).then_inc(dvec, 1)
                chain[0] += 1
            ve.wait_ge(dvec, chain[0])
            link(nc.vector.tensor_scalar(subln_c[:, 1:2], subln_c[:, 0:1], 1.0 - LAMBDA_INIT, None, ALU.mult))
            nc.vector.memset(fix[:, :], 0.0).then_inc(lam_ready, 1)

            def pooling(g):
                w = POOL_WINDOWS[g]
                u = mixT[:, H + g, :]
                ve.wait_ge(u_raw, G + g + 1)
                link(nc.vector.tensor_copy(win[0][:, PAD:PAD + 1], u[:, 0:1]))
                link(nc.vector.tensor_tensor(win[0][:, PAD + 1:PAD + SEQ], u[:, 1:SEQ], u[:, 0:SEQ - 1], ALU.add))
                a, reach = 0, 2
                while reach < w:
                    link(nc.vector.tensor_tensor(win[1 - a][:, PAD:PAD + SEQ], win[a][:, PAD:PAD + SEQ],
                                                 win[a][:, PAD - reach:PAD + SEQ - reach], ALU.add))
                    a, reach = 1 - a, 2 * reach
                link(nc.vector.tensor_tensor(fix[:, 0:w - 1], win[a][:, PAD:PAD + w - 1], inv_cnt[:, 0:w - 1], ALU.mult))
                link(nc.vector.tensor_tensor(resid[g % 2][:, 0:w - 1], fix[:, 0:w - 1], u[:, 0:w - 1], ALU.subtract))
                nc.vector.scalar_tensor_tensor(out=resid[g % 2][:, w - 1:SEQ], in0=win[a][:, PAD + w - 1:PAD + SEQ],
                                               scalar=1.0 / w, in1=u[:, w - 1:SEQ], op0=ALU.mult,
                                               op1=ALU.subtract).then_inc(res_ready, 1)
                ve.wait_ge(res_ready, g + 1)

            def res_low(g):
                ve.wait_ge(res_hi_ready, g + 1)
                nc.vector.tensor_tensor(res_lo[:, g % 2, :], resid[g % 2][:, :], res_hi[:, g % 2, :].bitcast(F32),
                                        ALU.subtract).then_inc(res_lo_ready, 1)
                ve.wait_ge(res_lo_ready, g + 1)

            def qk_low(h, n):
                ve.wait_ge(qk_hi, 4 * h + n + 1)
                hi, lo = ((q_hi, q_lo), (k_hi, k_lo))[n % 2]
                cols = slice((n // 2) * HALF, (n // 2 + 1) * HALF)
                nc.vector.tensor_tensor(lo[:, cols], bank(QK_BANK[n]), hi[:, cols].bitcast(F32),
                                        ALU.subtract).then_inc(qk_lo, 1)

            def t_low(h, group):
                kind, n, k0, nb = group
                i = t_index(h, group)
                ve.wait_ge(t_hi, i + 1)
                if kind == "V":
                    lo, hi = v_lo[:, k0:k0 + nb, :], v_hi[:, k0:k0 + nb, :]
                else:
                    cols = slice((n % 2) * P, (n % 2 + 1) * P)
                    lo, hi = attT_lo[:, k0:k0 + nb, cols], attT_hi[:, k0:k0 + nb, cols]
                nc.vector.tensor_tensor(lo, blocks(4 + i % 2, nb), hi.bitcast(F32), ALU.subtract).then_inc(t_lo, 1)

            def mask_max(h, s):
                n = NT * h + s
                L = (s + 1) * P
                ve.wait_ge(s_mm, n + 1)
                if n >= 2:
                    ve.wait_ge(t_mm, last_group(h, "T", s - 2) if s >= 2 else last_group(h - 1, "T", NT + s - 2))
                for r in range(2):
                    nc.vector.tensor_tensor_reduce(
                        out=prob[:, s % 2, r, 0:L],
                        in0=PS[:, 2 * r:2 * r + 2, :].rearrange("p b n -> p (b n)")[:, 0:L],
                        in1=mask[:, SEQ - L:SEQ], scale=1.0, scalar=LOWEST, op0=ALU.add, op1=ALU.max,
                        accum_out=smax[:, s % 2, r:r + 1]).then_inc(s_read, 1)
                ve.wait_ge(s_read, 2 * n + 2)
                nc.vector.tensor_scalar(nbias[:, s % 2, :], smax[:, s % 2, :], -SCALE, None, ALU.mult).then_inc(nb_ready, 1)

            def combine(h, s):
                n = NT * h + s
                L = (s + 1) * P
                ve.wait_ge(exp_done, 2 * n + 2)
                link(nc.vector.reciprocal(rsum[:, s % 2, :], lsum[:, s % 2, :]))
                link(nc.vector.tensor_scalar(prob[:, s % 2, 1, 0:L], prob[:, s % 2, 1, 0:L], rsum[:, s % 2, 1:2],
                                             neg_lam[:, 0:1], ALU.mult, ALU.mult))
                nc.vector.scalar_tensor_tensor(out=prob[:, s % 2, 0, 0:L], in0=prob[:, s % 2, 0, 0:L],
                                               scalar=rsum[:, s % 2, 0:1], in1=prob[:, s % 2, 1, 0:L],
                                               op0=ALU.mult, op1=ALU.add).then_inc(att_ready, 1)

            def o_norm(h, j):
                n = NPAIR * h + j
                ve.wait_ge(rstd_ready, n + 1)
                nc.vector.scalar_tensor_tensor(out=mixT[:, h, j * 2 * P:(j + 1) * 2 * P], in0=PS[:, 6, 0:2 * P],
                                               scalar=subln_c[:, 1:2], in1=o_rstd[:, :], op0=ALU.mult,
                                               op1=ALU.mult).then_inc(mix_ready, 1)

            ve.wait_ge(pads_set, 2)
            ve.wait_ge(cnt_set, PAD)
            pooling(0)
            for g in range(1, G):
                pooling(g)
                res_low(g - 1)
            res_low(G - 1)
            ve.wait_ge(lam_a, 1)
            link(nc.vector.tensor_scalar(neg_lam[:, 1:2], lam_exp[:, 1:2], -LAMBDA_INIT, None, ALU.add))
            link(nc.vector.tensor_tensor(neg_lam[:, 0:1], neg_lam[:, 1:2], lam_exp[:, 0:1], ALU.subtract))
            ve.wait_ge(mask_set, 1)
            qk_low(0, 0)
            for h in range(H):
                if h:
                    combine(h - 1, NT - 1)
                    for g in T_OF_STEP[8]:
                        t_low(h - 1, g)
                qk_low(h, 1)
                if h:
                    for g in T_OF_STEP[9]:
                        t_low(h - 1, g)
                    o_norm(h - 1, 2)
                for s in range(NT):
                    mask_max(h, s)
                    if s:
                        combine(h, s - 1)
                    for g in T_OF_STEP.get(s, []):
                        if g[0] == "T":
                            t_low(h, g)
                    if s == 1:
                        qk_low(h, 2)
                        if h:
                            o_norm(h - 1, 3)
                    if s == 2:
                        qk_low(h, 3)
                    if s in (5, 7):
                        o_norm(h, (s - 5) // 2)
                    for g in T_OF_STEP.get(s, []):
                        if g[0] == "V":
                            t_low(h, g)
                    if s == NT - 1 and h + 1 < H:
                        qk_low(h + 1, 0)

            def mix_low(t):
                ve.wait_ge(mx_hi, t + 1)
                nc.vector.tensor_tensor(w_lo[:, t % 4, :].rearrange("p (e n) -> p e n", e=KD),
                                        mixT[:, :, t * P:(t + 1) * P],
                                        w_hi[:, t % 4, :].bitcast(F32).rearrange("p (e n) -> p e n", e=KD),
                                        ALU.subtract).then_inc(mx_lo, 1)

            h = H - 1
            mix_low(0)
            mix_low(1)
            combine(h, NT - 1)
            for g in T_OF_STEP[8] + T_OF_STEP[9]:
                t_low(h, g)
            o_norm(h, 2)
            o_norm(h, 3)
            mix_low(2)
            mix_low(3)

            def x2_norm(t):
                ve.wait_ge(pow2, t + 1)
                nc.vector.scalar_tensor_tensor(out=xn2[:, t % 2, :], in0=x2[:, t, :], scalar=rs2[:, t:t + 1],
                                               in1=g2_row[:, :], op0=ALU.mult, op1=ALU.mult).then_inc(xn2_ready, 1)

            def lo_x2(t):
                for j in range(2):
                    ve.wait_ge(tr2_hi, 2 * t + j + 1)
                    cols = slice(t * P, (t + 1) * P)
                    nc.vector.tensor_tensor(h2T_lo[:, 4 * j:4 * j + 4, cols],
                                            blocks(4 * ((t // 2) % 2) + 2 * (t % 2) + j),
                                            h2T_hi[:, 4 * j:4 * j + 4, cols].bitcast(F32),
                                            ALU.subtract).then_inc(tr2_lo if t < NT - 2 else d_free, 1)

            ve.wait_ge(g2_here, 16)
            for p in range(NPAIR):
                ve.wait_ge(x2_here[p], 16)
                for i in range(2):
                    for half in range(2):
                        t = 2 * p + i
                        cols = slice(half * BANK, (half + 1) * BANK)
                        ve.wait_ge(o_mm, 2 * t + half + 1)
                        nc.vector.tensor_tensor(x2[:, t, cols], bank(4 * (p % 2) + 2 * i + half), x2[:, t, cols],
                                                ALU.add).then_inc(x2_add, 1)
                if p + 2 < NPAIR:
                    mix_low(2 * p + 4)
                    mix_low(2 * p + 5)
                x2_norm(2 * p)
                x2_norm(2 * p + 1)
                if p < NPAIR - 1:
                    lo_x2(2 * p)
                    lo_x2(2 * p + 1)

            def gate_up(s, c, half, slot):
                n = 2 * c + half
                ve.wait_ge(gu_mm, s * 8 + (2 * n + 2))
                ve.wait_ge(silu_done, s * 4 + (n + 1))
                nc.vector.tensor_tensor(gated[:, n % 2, :], silu_g[:, n % 2, :], bank(2 * half + 1),
                                        ALU.mult).then_inc(gated_ready, 1)
                ve.wait_ge(act_hi_ready, s * 4 + (n + 1))
                cols = slice(half * HALF, (half + 1) * HALF)
                nc.vector.tensor_tensor(act_lo[:, slot, c, cols], gated[:, n % 2, :],
                                        act_hi[:, slot, c, cols].bitcast(F32), ALU.subtract).then_inc(act_ready, 1)

            def add_down(s, t, half):
                n = 2 * t + half
                cols = slice(half * BANK, (half + 1) * BANK)
                ve.wait_ge(d_mm, s * 16 + (n + 1))
                nc.vector.tensor_tensor(x2[:, t, cols], bank(4 + n % 4), x2[:, t, cols], ALU.add).then_inc(d_free, 1)

            def ff_gate(s, slot, first=False):
                for c in range(2):
                    for half in range(2):
                        gate_up(s, c, half, slot)
                        if first and c == 0 and half == 0:
                            lo_x2(NT - 2)
                            lo_x2(NT - 1)

            def ff_down(s):
                for t in range(NT):
                    for half in range(2):
                        add_down(s, t, half)

            ff_gate(0, 0, first=True)
            with nc.Fori(0, STEPS // 2 - 1, engines=[ENG.DVE]) as i:
                ff_gate(i * 2 + 1, 1)
                ff_down(i * 2)
                ff_gate(i * 2 + 2, 0)
                ff_down(i * 2 + 1)
            ff_gate(STEPS - 2, 1)
            ff_down(STEPS - 3)
            ff_gate(STEPS - 1, 0)
            ff_down(STEPS - 2)

            def y_norm(t):
                ve.wait_ge(pow3, t + 1)
                nc.vector.scalar_tensor_tensor(out=x2[:, t, :], in0=x2[:, t, :], scalar=rs3[:, t:t + 1],
                                               in1=gf_row[:, :], op0=ALU.mult, op1=ALU.mult).then_inc(y_ready, 1)

            ve.wait_ge(gf_here, 16)
            for t in range(NT):
                for half in range(2):
                    add_down(STEPS - 1, t, half)
                if t >= 2:
                    y_norm(t - 2)
            y_norm(NT - 2)
            y_norm(NT - 1)

        @block.tensor
        def _(pe):
            def three(dst, a_hi, a_lo, b_hi, b_lo, start, stop):
                nc.tensor.matmul(dst, a_hi, b_hi, start=start, stop=False)
                nc.tensor.matmul(dst, a_hi, b_lo, start=False, stop=False)
                return nc.tensor.matmul(dst, a_lo, b_hi, start=False, stop=stop)

            def project(b, c, half, k0=0, k1=KD):
                for k in range(k0, k1):
                    ws = slice(k * P, (k + 1) * P)
                    cols = slice(half * HALF, (half + 1) * HALF)
                    mm = three(bank(b), w_hi[:, c, ws], w_lo[:, c, ws], hT_hi[:, k, cols], hT_lo[:, k, cols],
                               k == 0, k == KD - 1)
                return mm

            def x_tile(t):
                pe.wait_ge(xn_ready, t + 1)
                for j in range(2):
                    if t >= 2:
                        pe.wait_ge(tr1_lo, 2 * t + j - 3)
                    for k in range(4):
                        kk = 4 * j + k
                        tr = nc.tensor.transpose(bank(tr1_bank(t, j))[:, k * P:(k + 1) * P],
                                                 xn[:, t % 2, kk * P:(kk + 1) * P], ident[:, :])
                    tr.then_inc(tr1, 1)

            def u_group(n):
                half, g = divmod(n, G)
                if half == 0:
                    pe.wait_ge(wlo, blk_u(g))
                if n >= 4:
                    pe.wait_ge(u_raw, n - 3)
                project(n % 4, g, half).then_inc(u_mm, 1)

            pe.wait_ge(ident_set, 1)
            for t in range(4):
                x_tile(t)
            pe.wait_ge(tr1_lo, 8)
            u_group(0)
            x_tile(4)
            u_group(1)
            x_tile(5)
            u_group(2)
            x_tile(6)
            x_tile(7)
            u_group(3)
            pe.wait_ge(tr1_lo, 2 * NT)
            for n in range(4, 8):
                u_group(n)

            def y_group(g):
                if g == 0:
                    pe.wait_ge(wlo, BLK_PW)
                    pe.wait_ge(u_raw, 2 * G)
                if g >= 2:
                    pe.wait_ge(y_out, 2 * (g - 1))
                pe.wait_ge(res_lo_ready, g + 1)
                for half in range(2):
                    cols = slice(half * HALF, (half + 1) * HALF)
                    three(bank(y_bank(g, half)), pw_hi[:, g, :], pw_lo[:, g, :], res_hi[:, g % 2, cols],
                          res_lo[:, g % 2, cols], True, True).then_inc(y_mm, 1)

            def qk_part(h, n, k0=0, k1=KD):
                if k0 == 0:
                    if n < 2:
                        pe.wait_ge(wlo, blk_qkv(h, n))
                    if n == 0 and h:
                        pe.wait_ge(qk_lo, 4 * h)
                    if n == 1 and h:
                        pe.wait_ge(s_read, 2 * NT * h)
                    if n == 3:
                        pe.wait_ge(v_raw, 2 * h + 1)
                mm = project(QK_BANK[n], n % 2, n // 2, k0, k1)
                if k1 == KD:
                    mm.then_inc(qk_mm, 1)

            def v_group(h, half):
                if half == 0:
                    pe.wait_ge(wlo, blk_qkv(h, 2))
                    pe.wait_ge(qk_lo, 4 * h + 1)
                elif h == 0:
                    pe.wait_ge(y_out, 2 * G)
                project(V_BANK[half], 2, half).then_inc(v_mm, 1)

            def scores(h, s):
                n = NT * h + s
                L = (s + 1) * P
                if n:
                    pe.wait_ge(s_read, 2 * n)
                if s == 0:
                    pe.wait_ge(qk_lo, 4 * h + 2)
                if s == 4:
                    pe.wait_ge(qk_lo, 4 * h + 4)
                    pe.wait_ge(v_raw, 2 * h + 2)
                qs = slice(s * P, (s + 1) * P)
                for k0 in range(0, L, BANK):
                    w = min(BANK, L - k0)
                    ks = slice(k0, k0 + w)
                    for a, b, first, last in ((q_hi, k_hi, True, False), (q_hi, k_lo, False, False),
                                              (q_lo, k_hi, False, True)):
                        for r in range(2):
                            rows = slice(r * HD, (r + 1) * HD)
                            mm = nc.tensor.matmul(PS[:, 2 * r + k0 // BANK, 0:w], a[rows, qs], b[rows, ks],
                                                  start=first, stop=last)
                mm.then_inc(s_mm, 1)

            def transposes(h, group):
                kind, n, k0, nb = group
                i = t_index(h, group)
                if i >= 2:
                    pe.wait_ge(t_lo, i - 1)
                elif i == 0:
                    pe.wait_ge(y_out, 2 * G)
                if kind == "V":
                    pe.wait_ge(v_raw, 2 * h + n + 1)
                else:
                    pe.wait_ge(att_ready, NT * h + n + 1)
                for b in range(nb):
                    kb = k0 + b
                    ks = slice(kb * P, (kb + 1) * P)
                    src = vT[:, ks] if kind == "V" else prob[:, n % 2, 0, ks]
                    tr = nc.tensor.transpose(bank(4 + i % 2)[:, b * P:(b + 1) * P], src, ident[:, :])
                tr.then_inc(t_mm, 1)

            def values(h, j):
                n = NPAIR * h + j
                if n:
                    pe.wait_ge(mix_ready, n)
                pe.wait_ge(t_lo, max(last_group(h, "T", 2 * j + 1), last_group(h, "V", 1 if j >= 2 else 0)))
                for kb in range(2 * j + 2):
                    c0 = 0 if kb <= 2 * j else P
                    mm = three(PS[:, 6, c0:2 * P], v_hi[:, kb, :], v_lo[:, kb, :], attT_hi[:, kb, c0:2 * P],
                               attT_lo[:, kb, c0:2 * P], kb == 0, kb == 2 * j + 1)
                mm.then_inc(pv_mm, 1)

            def square_sum(h, j):
                n = NPAIR * h + j
                pe.wait_ge(osq_ready, n + 1)
                nc.tensor.matmul(PS[:, 6, 2 * P:4 * P], ones[:, :], o_sq[:, :], start=True, stop=True).then_inc(ss_mm, 1)

            pe.wait_ge(ones_set, 1)
            y_group(0)
            y_group(1)
            qk_part(0, 0)
            y_group(2)
            for h in range(H):
                if h:
                    qk_part(h, 1, 0, KD // 2)
                    for g in T_OF_STEP[8]:
                        transposes(h - 1, g)
                    values(h - 1, 2)
                    qk_part(h, 1, KD // 2, KD)
                    for g in T_OF_STEP[9]:
                        transposes(h - 1, g)
                    square_sum(h - 1, 2)
                else:
                    qk_part(h, 1)
                    y_group(3)
                for s in range(NT):
                    scores(h, s)
                    if s == 3:
                        v_group(h, 1)
                    for g in T_OF_STEP.get(s, []):
                        if g[0] == "T":
                            transposes(h, g)
                    if s == 0:
                        v_group(h, 0)
                        if h:
                            values(h - 1, 3)
                    if s == 1:
                        qk_part(h, 2)
                        if h:
                            square_sum(h - 1, 3)
                    if s == 2:
                        qk_part(h, 3)
                    if s >= 4 and h + 1 < H:
                        qk_part(h + 1, 0, 2 * (s - 4), 2 * (s - 3))
                    if s in (4, 6):
                        values(h, (s - 4) // 2)
                    if s in (5, 7):
                        square_sum(h, (s - 5) // 2)
                    for g in T_OF_STEP.get(s, []):
                        if g[0] == "V":
                            transposes(h, g)

            def out_project(p, n0, n1):
                for n in range(n0, n1):
                    e = WO_ORDER[n]
                    if p == 0:
                        pe.wait_ge(wo_lo, n + 1)
                    es = slice(e * P, (e + 1) * P)
                    for i in range(2):
                        c = (2 * p + i) % 4
                        for half in range(2):
                            cols = slice(half * BANK, (half + 1) * BANK)
                            mm = three(bank(4 * (p % 2) + 2 * i + half), w_hi[:, c, es], w_lo[:, c, es],
                                       wout_hi[:, e, cols], wout_lo[:, e, cols], n == 0, n == KD - 1)
                            if n == KD - 1:
                                mm.then_inc(o_mm, 1)

            def x2_tiles(p):
                for t in (2 * p, 2 * p + 1):
                    pe.wait_ge(xn2_ready, t + 1)
                    for j in range(2):
                        b = 4 * (p % 2) + 2 * (t % 2) + j
                        for k in range(4):
                            kk = 4 * j + k
                            tr = nc.tensor.transpose(bank(b)[:, k * P:(k + 1) * P], xn2[:, t % 2, kk * P:(kk + 1) * P],
                                                     ident[:, :])
                        tr.then_inc(tr2, 1)

            h = H - 1
            pe.wait_ge(s_read, 2 * NT * H)
            pe.wait_ge(mx_lo, 2)
            for g in T_OF_STEP[8]:
                transposes(h, g)
            values(h, 2)
            out_project(0, 0, 2)
            for g in T_OF_STEP[9]:
                transposes(h, g)
            square_sum(h, 2)
            out_project(0, 2, 4)
            values(h, 3)
            out_project(0, 4, 6)
            square_sum(h, 3)
            out_project(0, 6, 8)
            for p in range(1, NPAIR):
                pe.wait_ge(mx_lo, 2 * p + 2)
                if p == 1:
                    pe.wait_ge(t_lo, H * T_PER_HEAD)
                    pe.wait_ge(mix_ready, H * NPAIR)
                else:
                    pe.wait_ge(tr2_lo, 4 * (p - 1))
                out_project(p, 0, 4)
                x2_tiles(p - 1)
                out_project(p, 4, 8)

            def gate_up(s, c, half):
                n = 2 * c + half
                if not (isinstance(s, int) and s == 0 and n < 2):
                    pe.wait_ge(gated_ready, s * 4 + (n - 1))
                for kind in range(2):
                    slot = 2 * c + kind
                    if half == 0:
                        pe.wait_ge(fw_lo, s * 4 + (slot + 1))
                    cols = slice(half * HALF, (half + 1) * HALF)
                    for k in range(KD):
                        ws = slice(k * P, (k + 1) * P)
                        mm = three(bank(2 * half + kind), w_hi[:, slot, ws], w_lo[:, slot, ws],
                                   h2T_hi[:, k, cols], h2T_lo[:, k, cols], k == 0, k == KD - 1)
                    mm.then_inc(gu_mm, 1)

            def ff_gate(s):
                for c in range(2):
                    for half in range(2):
                        gate_up(s, c, half)

            def ff_down(s, slot):
                pe.wait_ge(act_ready, s * 4 + 4)
                pe.wait_ge(fd_lo, s + 1)
                for t in range(NT):
                    ts = slice(t * P, (t + 1) * P)
                    for half in range(2):
                        n = 2 * t + half
                        pe.wait_ge(d_free, s * 16 + (n + 1))
                        cols = slice(half * BANK, (half + 1) * BANK)
                        for c in range(2):
                            mm = three(bank(4 + n % 4), act_hi[:, slot, c, ts], act_lo[:, slot, c, ts],
                                       dn_hi[:, c, cols], dn_lo[:, c, cols], c == 0, c == 1)
                        mm.then_inc(d_mm, 1)

            pe.wait_ge(tr2_lo, 4 * (NPAIR - 1))
            gate_up(0, 0, 0)
            x2_tiles(NPAIR - 1)
            pe.wait_ge(d_free, 4)
            gate_up(0, 0, 1)
            gate_up(0, 1, 0)
            gate_up(0, 1, 1)
            with nc.Fori(0, STEPS // 2 - 1, engines=[ENG.PE]) as i:
                ff_gate(i * 2 + 1)
                ff_down(i * 2, 0)
                ff_gate(i * 2 + 2)
                ff_down(i * 2 + 1, 1)
            ff_gate(STEPS - 2)
            ff_down(STEPS - 3, 0)
            ff_gate(STEPS - 1)
            ff_down(STEPS - 2, 1)
            ff_down(STEPS - 1, 0)


_INS = ["x", "norm1_g", "w_in", "lam_qk", "subln_g", "pool_w", "pool_scale", "w_out",
        "norm2_g", "w_gate", "w_up", "w_down", "final_g"]


def kernel(**inputs):
    import numpy as _np
    import concourse.bacc as _bacc
    from concourse import mybir as _mybir
    from concourse.bass_utils import run_bass_kernel_spmd as _run

    nc = _bacc.Bacc("TRN2", target_bir_lowering=False, num_devices=1, dynamic_dma_scratch_size=DMA_SCRATCH)
    arrays, args = {}, []
    for name in _INS:
        a = _np.ascontiguousarray(inputs[name])
        arrays[f"in_{name}_dram"] = a
        args.append(nc.dram_tensor(f"in_{name}_dram", a.shape, _mybir.dt.from_np(a.dtype), kind="ExternalInput").ap())
    shape = _np.shape(inputs["x"])
    args.append(nc.dram_tensor("out_0_dram", shape, _mybir.dt.float32, kind="ExternalOutput").ap())
    hybrid_block(nc, *args)
    r = _run(nc, [arrays], core_ids=[0])
    return r.results[0]["out_0_dram"]
```

```python
import math
from contextlib import ExitStack

import concourse.bass as bass
from concourse import mybir

F32 = mybir.dt.float32
F32R = mybir.dt.float32r
ALU = mybir.AluOpType
ACT = mybir.ActivationFunctionType
ENG = mybir.EngineType

P = 128
BANK = 512
POOL_WINDOWS = (2, 4, 8, 16)
NORM_EPS = 1e-5
LAMBDA_INIT = 0.8 - 0.6 * math.exp(-0.3 * 0)
MASKED = -1.0e30
LOWEST = -3.0e38
DMA_SCRATCH = 1024
KIB = 1024


def hybrid_block(nc, x, norm1_g, w_in, lam_qk, subln_g, pool_w, pool_scale, w_out,
                 norm2_g, w_gate, w_up, w_down, final_g, out):
    _, SEQ, D = x.shape
    HD = lam_qk.shape[2]
    VD = subln_g.shape[1]
    POOL = pool_scale.shape[1]
    G = POOL // P
    ATTN = D - POOL
    H = ATTN // VD
    FF = w_gate.shape[2]
    NT = SEQ // P
    KD = D // P
    NF = FF // P
    STEPS = NF // 2
    HALF = SEQ // 2
    assert VD == P == 2 * HD and HALF == BANK and D == 2 * BANK and NT == KD == 8 and H == G == 4
    assert NF % 2 == 0 and STEPS % 2 == 1
    SCALE = HD ** -0.5

    with ExitStack() as ctx:
        def sem(name):
            return ctx.enter_context(nc.semaphore(name))

        R0 = 2 * KIB
        R1 = R0 + 64 * KIB
        R2 = R1 + 32 * KIB
        R3 = R2 + 64 * KIB
        RC = R3 + 48 * KIB

        def at(name, offset, shape, dt=F32):
            return nc.alloc_sbuf_tensor_at(name, [P, *shape], dt, offset=offset)

        hT_hi = at("hT_hi", R0, [KD, SEQ], F32R)
        hT_lo = at("hT_lo", R0 + 32 * KIB, [KD, SEQ], F32R)
        wout_hi = at("wout_hi", R0, [KD, D], F32R)
        wout_lo = at("wout_lo", R0 + 32 * KIB, [KD, D], F32R)
        act_hi = at("act_hi", R0, [2, 2, SEQ], F32R)
        act_lo = at("act_lo", R0 + 16 * KIB, [2, 2, SEQ], F32R)
        dn_hi = at("dn_hi", R0 + 32 * KIB, [2, D], F32R)
        dn_lo = at("dn_lo", R0 + 40 * KIB, [2, D], F32R)
        dn_raw = at("dn_raw", R0 + 48 * KIB, [2, D])
        silu_g = at("silu_g", R0 + 56 * KIB, [2, BANK])
        gated = at("gated", R0 + 60 * KIB, [2, BANK])

        x_in = at("x_in", R1, [NT, D])
        mixT = at("mixT", R1, [KD, SEQ])
        h2T_hi = at("h2T_hi", R1, [KD, SEQ], F32R)

        q_hi = at("q_hi", R2, [SEQ], F32R)
        q_lo = at("q_lo", R2 + 4 * KIB, [SEQ], F32R)
        k_hi = at("k_hi", R2 + 8 * KIB, [SEQ], F32R)
        k_lo = at("k_lo", R2 + 12 * KIB, [SEQ], F32R)
        v_hi = at("v_hi", R2 + 16 * KIB, [NT, P], F32R)
        v_lo = at("v_lo", R2 + 20 * KIB, [NT, P], F32R)
        vT = at("vT", R2 + 24 * KIB, [SEQ])
        prob = at("prob", R2 + 28 * KIB, [2, 2, SEQ])
        attT_hi = at("attT_hi", R2 + 44 * KIB, [NT, 2 * P], F32R)
        attT_lo = at("attT_lo", R2 + 52 * KIB, [NT, 2 * P], F32R)
        o_sq = at("o_sq", R2 + 60 * KIB, [2 * P])
        o_rstd = at("o_rstd", R2 + 61 * KIB, [2 * P])
        junk = at("junk", R2 + 24 * KIB, [D])
        xn = at("xn", R2 + 28 * KIB, [2, D])
        PAD = max(POOL_WINDOWS)
        win = [at(f"win{i}", R2 + (28 + 5 * i) * KIB, [PAD + SEQ]) for i in range(2)]
        resid = [at("resid0", R2 + 38 * KIB, [SEQ]), at("resid1", R2 + 24 * KIB, [SEQ])]
        pw_raw = at("pw_raw", R2 + 16 * KIB, [G, P])
        pw_hi = at("pw_hi", R2 + 18 * KIB, [G, P], F32R)
        pw_lo = at("pw_lo", R2 + 20 * KIB, [G, P], F32R)
        res_hi = at("res_hi", R2 + 44 * KIB, [2, SEQ], F32R)
        res_lo = at("res_lo", R2 + 52 * KIB, [2, SEQ], F32R)
        x2 = at("x2", R2, [NT, D])
        h2T_lo = at("h2T_lo", R2 + 32 * KIB, [KD, SEQ], F32R)

        w_raw = at("w_raw", R3, [4, D])
        w_hi = at("w_hi", R3 + 16 * KIB, [4, D], F32R)
        w_lo = at("w_lo", R3 + 32 * KIB, [4, D], F32R)

        g1_in = at("g1_in", R3 + 44 * KIB, [D])
        g1_row = at("g1_row", RC, [D])
        mask = at("mask", RC + 4 * KIB, [SEQ])
        xn2 = at("xn2", RC, [2, D])
        g2_row = at("g2_row", RC + 8 * KIB, [D])
        gf_row = at("gf_row", RC + 8 * KIB, [D])
        ident = at("ident", RC + 12 * KIB, [P])
        ones = at("ones", RC + 12 * KIB + 512, [P])
        lam_in = at("lam_in", R2, [4, HD])
        lam_pr = at("lam_pr", R2 + KIB, [2, HD])
        small = RC + 13 * KIB - 1536
        lam_sum = at("lam_sum", small + 1536, [2])
        lam_exp = at("lam_exp", small + 1568, [2])
        neg_lam = at("neg_lam", small + 1600, [2])
        subln_c = at("subln_c", small + 1632, [2])
        pscale_c = at("pscale_c", small + 1664, [G])
        inv_cnt = at("inv_cnt", small + 1696, [PAD])
        fix = at("fix", small + 1760, [PAD])
        eps_c = at("eps_c", small + 1824, [1])
        mhalf = at("mhalf", small + 1856, [NT])
        ss1 = at("ss1", small + 1888, [NT])
        rs1 = at("rs1", small + 1920, [NT])
        ss2 = at("ss2", small + 1952, [NT])
        rs2 = at("rs2", small + 1984, [NT])
        ss3 = at("ss3", small + 2016, [2 * NT])
        rs3 = at("rs3", small + 2080, [NT])
        smax = at("smax", small + 2112, [2, 2])
        nbias = at("nbias", small + 2144, [2, 2])
        lsum = at("lsum", small + 2176, [2, 2])
        rsum = at("rsum", small + 2208, [2, 2])
        ms = at("ms", small + 2240, [NT])

        PS = ctx.enter_context(nc.psum_tensor("PS", [P, 8, BANK], F32))

        def bank(b):
            return PS[:, b, :]

        def blocks(b, n=4):
            return PS[:, b, 0:n * P].rearrange("p (n c) -> p n c", c=P)

        x_in_here = [sem(f"x_in_here{t}") for t in range(NT)]
        x2_here = [sem(f"x2_here{i}") for i in range(NT // 2)]
        small_here, g1_here, g2_here, gf_here = sem("small_here"), sem("g1_here"), sem("g2_here"), sem("gf_here")
        raw_here = [sem(f"raw_here{i}") for i in range(4)]
        pw_here = sem("pw_here")
        dn_here = sem("dn_here")
        ident_set, mhalf_set, ones_set, eps_set, pads_set, mask_set, cnt_set = (
            sem("ident_set"), sem("mhalf_set"), sem("ones_set"), sem("eps_set"), sem("pads_set"),
            sem("mask_set"), sem("cnt_set"))
        dvec = sem("dvec")
        lam_ready, lam_a = sem("lam_ready"), sem("lam_a")
        sq1, pow1 = sem("sq1"), sem("pow1")
        poolc = sem("poolc")
        xn_ready = sem("xn_ready")
        g1_mm, g1_set = sem("g1_mm"), sem("g1_set")
        tr1, tr1_hi, tr1_lo = sem("tr1"), sem("tr1_hi"), sem("tr1_lo")
        whi, wlo = sem("whi"), sem("wlo")
        u_mm, u_raw = sem("u_mm"), sem("u_raw")
        res_ready, res_hi_ready, res_lo_ready = sem("res_ready"), sem("res_hi_ready"), sem("res_lo_ready")
        y_mm, y_out = sem("y_mm"), sem("y_out")
        qk_mm, qk_hi, qk_lo = sem("qk_mm"), sem("qk_hi"), sem("qk_lo")
        v_mm, v_raw = sem("v_mm"), sem("v_raw")
        s_mm, s_read, nb_ready, exp_done, att_ready = (
            sem("s_mm"), sem("s_read"), sem("nb_ready"), sem("exp_done"), sem("att_ready"))
        t_mm, t_hi, t_lo = sem("t_mm"), sem("t_hi"), sem("t_lo")
        pv_mm, osq_ready, ss_mm, ln_done, rstd_ready, mix_ready = (
            sem("pv_mm"), sem("osq_ready"), sem("ss_mm"), sem("ln_done"), sem("rstd_ready"), sem("mix_ready"))
        mx_hi, mx_lo = sem("mx_hi"), sem("mx_lo")
        wo_hi, wo_lo = sem("wo_hi"), sem("wo_lo")
        o_mm, x2_add, sq2, pow2, xn2_ready = sem("o_mm"), sem("x2_add"), sem("sq2"), sem("pow2"), sem("xn2_ready")
        tr2, tr2_hi, tr2_lo = sem("tr2"), sem("tr2_hi"), sem("tr2_lo")
        fw_hi, fw_lo, fd_hi, fd_lo = sem("fw_hi"), sem("fw_lo"), sem("fd_hi"), sem("fd_lo")
        gu_mm, silu_done, gated_ready, act_hi_ready, act_ready = (
            sem("gu_mm"), sem("silu_done"), sem("gated_ready"), sem("act_hi_ready"), sem("act_ready"))
        d_mm = sem("d_mm")
        d_free = sem("d_free")
        sq3, pow3, y_ready, out_done = sem("sq3"), sem("pow3"), sem("y_ready"), sem("out_done")

        def blk_u(g):
            return g + 1
        BLK_PW = G + 1

        def blk_qkv(h, c):
            return G + 1 + 3 * h + c + 1

        def t_groups(qt):
            n = qt + 1
            return [("T", qt, k0, min(4, n - k0)) for k0 in range(0, n, 4)]
        V0, V1 = ("V", 0, 0, 4), ("V", 1, 4, 4)

        def t_of_step(h, s):
            groups = t_groups(s - 2) if s >= 2 else []
            if s == 1:
                groups = [V0]
            if s == V1_STEP[h]:
                groups = groups + [V1]
            return groups
        V1_STEP = [4] * (H - 1) + [7]

        def in_step(h, s):
            return [g for g in t_of_step(h, s) if g != V0 and not (g == V1 and h == H - 1)]
        T_SEQ = [(h, g) for h in range(H) for s in range(NT + 2) for g in t_of_step(h, s)]

        def t_index(h, group):
            return T_SEQ.index((h, group))

        def last_group(h, kind, n):
            return max(i for i, (head, g) in enumerate(T_SEQ) if head == h and g[0] == kind and g[1] == n) + 1

        def tr1_bank(t, j):
            return 4 + 2 * (t % 2) + j

        def u_bank(n):
            return (n + 2) % 4

        QK_BANK = (7, 0, 3, 7)

        def v_bank(h, half):
            return 1 if half and h + 1 < H else 7

        def y_bank(g, half):
            return ((6, 1), (4, 5))[g % 2][half]

        NPAIR = NT // 2
        WO_ORDER = list(range(H, KD)) + list(range(H))

        def o_bank(t, half):
            return (2 * (t % 4) + half + 7) % 8

        def tr2_bank(t, j):
            return o_bank(t, j) if t < NT - 2 else 4 + 2 * (t % 2) + j

        def wo_slot(n):
            return (n + 3) % 4

        block = ctx.enter_context(nc.Block())

        @block.sync
        def _(sp):
            xt = x[0].rearrange("(t p) d -> p t d", p=P)
            w_in_v = w_in[0].rearrange("(k p) n -> p k n", p=P)
            w_out_v = w_out[0].rearrange("(k p) n -> p k n", p=P)
            gate_v = w_gate[0].rearrange("(k p) n -> p k n", p=P)
            up_v = w_up[0].rearrange("(k p) n -> p k n", p=P)
            down_v = w_down[0].rearrange("(f p) n -> p f n", p=P)
            slot = [w_raw[:, c, :].rearrange("p (k n) -> p k n", k=KD) for c in range(4)]

            def load_x(t):
                sp.dma_start(x_in[:, t, :], xt[:, t, :]).then_inc(x_in_here[t], 16)

            def load_in(c, col):
                sp.dma_start(slot[c], w_in_v[:, :, col:col + P]).then_inc(raw_here[c], 16)

            sp.dma_start(g1_in[0:1, :], norm1_g[0:1, :]).then_inc(g1_here, 16)
            load_x(0)
            load_x(1)
            load_in(0, 3 * ATTN)
            load_x(2)
            load_in(1, 3 * ATTN + P)
            load_x(3)
            load_x(4)
            load_x(5)
            load_in(2, 3 * ATTN + 2 * P)
            load_x(6)
            load_in(3, 3 * ATTN + 3 * P)
            load_x(7)
            sp.dma_start(pw_raw[:, :, :], pool_w[0].rearrange("g c n -> c g n")).then_inc(pw_here, 16)
            sp.dma_start(lam_in[:, :, :], lam_qk[0:1, :, :].to_broadcast([P, 4, HD])).then_inc(small_here, 16)
            sp.dma_start(subln_c[:, 0:1], subln_g.rearrange("a (d b) -> (a d) b", b=1)).then_inc(small_here, 16)
            for g in range(G):
                sp.dma_start(pscale_c[:, g:g + 1], pool_scale[0].rearrange("(g p b) -> g p b", p=P, b=1)[g])\
                  .then_inc(small_here, 16)
            sp.dma_start(g2_row[:, :], norm2_g[0:1, :].to_broadcast([P, D])).then_inc(g2_here, 16)
            for h in range(H):
                for c in range(3):
                    sp.wait_ge(wlo, blk_u(c) if h == 0 else blk_qkv(h - 1, c))
                    load_in(c, c * ATTN + h * P)
            for n, e in enumerate(WO_ORDER):
                if n == 0:
                    sp.wait_ge(wlo, blk_u(3))
                elif n < 4:
                    sp.wait_ge(wlo, blk_qkv(H - 1, wo_slot(n)))
                else:
                    sp.wait_ge(wo_lo, n - 3)
                sp.dma_start(w_raw[:, wo_slot(n), :], w_out_v[:, e, :]).then_inc(raw_here[wo_slot(n)], 16)
            sp.wait_ge(s_mm, H * NT)
            for i in range(NT // 2):
                if i == 2:
                    sp.wait_ge(pv_mm, H * NPAIR)
                    sp.wait_ge(t_mm, len(T_SEQ))
                sp.dma_start(x2[:, 2 * i:2 * i + 2, :], xt[:, 2 * i:2 * i + 2, :]).then_inc(x2_here[i], 16)

            def load_gu(s, c, kind):
                src = (gate_v, up_v)[kind]
                cols = bass.ds(s * 2 * P + c * P, P) if not isinstance(s, int) else slice(s * 2 * P + c * P, s * 2 * P + c * P + P)
                sp.dma_start(slot[2 * c + kind], src[:, :, cols]).then_inc(raw_here[2 * c + kind], 16)

            for c in range(4):
                n = max(m for m in range(KD) if wo_slot(m) == c)
                sp.wait_ge(wo_lo, n + 1)
                load_gu(0, c // 2, c % 2)
            sp.wait_ge(o_mm, 4 * NPAIR)
            sp.dma_start(dn_raw[:, :, :], down_v[:, 0:2, :]).then_inc(dn_here, 16)
            sp.wait_ge(xn2_ready, NT)
            sp.dma_start(gf_row[:, :], final_g.rearrange("(a d) -> a d", a=1).to_broadcast([P, D])).then_inc(gf_here, 16)
            with nc.Fori(1, STEPS, engines=[ENG.SP]) as s:
                for c in range(4):
                    sp.wait_ge(fw_lo, s * 4 + (c - 3))
                    load_gu(s, c // 2, c % 2)
                sp.wait_ge(fd_lo, s)
                sp.dma_start(dn_raw[:, :, :], down_v[:, bass.ds(s * 2, 2), :]).then_inc(dn_here, 16)
            for t in range(NT - 1):
                sp.wait_ge(y_ready, t + 1)
                sp.dma_start(out[0, t * P:(t + 1) * P, :], x2[:, t, :]).then_inc(out_done, 16)
            for half in range(2):
                cols = slice(half * BANK, (half + 1) * BANK)
                sp.wait_ge(y_ready, NT + half)
                sp.dma_start(out[0, (NT - 1) * P:NT * P, cols], x2[:, NT - 1, cols]).then_inc(out_done, 16)
            sp.wait_ge(out_done, 16 * (NT + 1))

        @block.gpsimd
        def _(gp):
            chain = [0]

            def link(ins):
                chain[0] += 1
                ins.then_inc(poolc, 1)
                gp.wait_ge(poolc, chain[0])

            link(nc.gpsimd.memset(ident[:, :], 0.0))
            nc.gpsimd.affine_select(out=ident[:, :], in_=ident[:, :], compare_op=ALU.not_equal, fill=1.0,
                                    base=0, pattern=[[-1, P]], channel_multiplier=1).then_inc(ident_set, 1)
            nc.gpsimd.memset(mhalf[:, :], -0.5).then_inc(mhalf_set, 1)
            gp.wait_ge(mhalf_set, 1)

            nc.gpsimd.memset(ones[:, :], 1.0).then_inc(ones_set, 1)
            nc.gpsimd.memset(eps_c[:, :], NORM_EPS).then_inc(eps_set, 1)
            for j in range(PAD):
                nc.gpsimd.memset(inv_cnt[:, j:j + 1], 1.0 / (j + 1)).then_inc(cnt_set, 1)
            link(nc.gpsimd.memset(mask[:, :], 0.0))
            nc.gpsimd.affine_select(out=mask[:, SEQ - P:SEQ], in_=mask[:, SEQ - P:SEQ], compare_op=ALU.is_ge,
                                    fill=MASKED, base=0, pattern=[[-1, P]], channel_multiplier=1).then_inc(mask_set, 1)

            def low(c, n):
                gp.wait_ge(whi, n)
                nc.gpsimd.tensor_tensor(w_lo[:, c, :], w_raw[:, c, :], w_hi[:, c, :].bitcast(F32),
                                        ALU.subtract).then_inc(wlo, 1)

            def pow_x(t):
                gp.wait_ge(sq1, t + 1)
                link(nc.gpsimd.tensor_scalar(ms[:, t:t + 1], ss1[:, t:t + 1], 1.0 / D, NORM_EPS, ALU.mult, ALU.add))
                nc.gpsimd.tensor_tensor(rs1[:, t:t + 1], ms[:, t:t + 1], mhalf[:, 0:1], ALU.pow).then_inc(pow1, 1)

            pow_x(0)
            pow_x(1)
            low(0, blk_u(0))
            pow_x(2)
            low(1, blk_u(1))
            pow_x(3)
            pow_x(4)
            pow_x(5)
            low(2, blk_u(2))
            pow_x(6)
            pow_x(7)
            low(3, blk_u(3))
            gp.wait_ge(whi, BLK_PW)
            nc.gpsimd.tensor_tensor(pw_lo[:, :, :], pw_raw[:, :, :], pw_hi[:, :, :].bitcast(F32),
                                    ALU.subtract).then_inc(wlo, 1)
            gp.wait_ge(tr1, 2 * NT)
            for i in range(2):
                nc.gpsimd.memset(win[i][:, 0:PAD], 0.0).then_inc(pads_set, 1)
            for h in range(H):
                for c in range(3):
                    low(c, blk_qkv(h, c))
            for n, e in enumerate(WO_ORDER):
                gp.wait_ge(wo_hi, n + 1)
                nc.gpsimd.tensor_tensor(wout_lo[:, e, :], w_raw[:, wo_slot(n), :], wout_hi[:, e, :].bitcast(F32),
                                        ALU.subtract).then_inc(wo_lo, 1)

            def pow_x2(t):
                gp.wait_ge(sq2, t + 1)
                link(nc.gpsimd.tensor_scalar(ms[:, t:t + 1], ss2[:, t:t + 1], 1.0 / D, NORM_EPS, ALU.mult, ALU.add))
                nc.gpsimd.tensor_tensor(rs2[:, t:t + 1], ms[:, t:t + 1], mhalf[:, 0:1], ALU.pow).then_inc(pow2, 1)

            def low_gu(s, c):
                gp.wait_ge(fw_hi, s * 4 + c + 1)
                nc.gpsimd.tensor_tensor(w_lo[:, c, :], w_raw[:, c, :], w_hi[:, c, :].bitcast(F32),
                                        ALU.subtract).then_inc(fw_lo, 1)

            def low_dn(s):
                gp.wait_ge(fd_hi, s + 1)
                nc.gpsimd.tensor_tensor(dn_lo[:, :, :], dn_raw[:, :, :], dn_hi[:, :, :].bitcast(F32),
                                        ALU.subtract).then_inc(fd_lo, 1)

            for t in range(NT - 2):
                pow_x2(t)
            low_gu(0, 0)
            low_gu(0, 1)
            pow_x2(NT - 2)
            pow_x2(NT - 1)
            low_gu(0, 2)
            low_gu(0, 3)
            with nc.Fori(1, STEPS, engines=[ENG.Pool]) as s:
                for c in range(4):
                    low_gu(s, c)
                low_dn(s - 1)
            gp.wait_ge(fd_hi, STEPS)
            nc.gpsimd.tensor_tensor(w_lo[:, 0:2, :], dn_raw[:, :, :], w_hi[:, 0:2, :].bitcast(F32),
                                    ALU.subtract).then_inc(fd_lo, 1)
            for t in range(NT):
                gp.wait_ge(sq3, 2 * t + 2)
                link(nc.gpsimd.tensor_tensor(ms[:, t:t + 1], ss3[:, 2 * t:2 * t + 1], ss3[:, 2 * t + 1:2 * t + 2], ALU.add))
                link(nc.gpsimd.tensor_scalar(ms[:, t:t + 1], ms[:, t:t + 1], 1.0 / D, NORM_EPS, ALU.mult, ALU.add))
                nc.gpsimd.tensor_tensor(rs3[:, t:t + 1], ms[:, t:t + 1], mhalf[:, 0:1], ALU.pow).then_inc(pow3, 1)

        @block.scalar
        def _(act):
            nc.scalar.preload_act_table_set("natural_log_exp_and_others")

            def split_hi(c, count):
                act.wait_ge(raw_here[c], 16 * count)
                nc.scalar.copy(w_hi[:, c, :], w_raw[:, c, :]).then_inc(whi, 1)

            def hi_x(t):
                for j in range(2):
                    act.wait_ge(tr1, 2 * t + j + 1)
                    nc.scalar.copy(hT_hi[:, 4 * j:4 * j + 4, t * P:(t + 1) * P],
                                   blocks(tr1_bank(t, j))).then_inc(tr1_hi, 1)

            def square_x(t):
                act.wait_ge(x_in_here[t], 16)
                if t:
                    act.wait_ge(sq1, t)
                nc.scalar.activation(junk[:, :], x_in[:, t, :], ACT.Square, accum_out=ss1[:, t:t + 1]).then_inc(sq1, 1)

            square_x(0)
            square_x(1)
            split_hi(0, 1)
            hi_x(0)
            square_x(2)
            hi_x(1)
            split_hi(1, 1)
            square_x(3)
            square_x(4)
            hi_x(2)
            hi_x(3)
            square_x(5)
            split_hi(2, 1)
            hi_x(4)
            square_x(6)
            square_x(7)
            split_hi(3, 1)
            hi_x(5)
            act.wait_ge(pw_here, 16)
            nc.scalar.copy(pw_hi[:, :, :], pw_raw[:, :, :]).then_inc(whi, 1)
            hi_x(6)
            hi_x(7)

            def u_copy(n):
                half, g = divmod(n, G)
                act.wait_ge(u_mm, n + 1)
                nc.scalar.copy(mixT[:, H + g, half * HALF:(half + 1) * HALF], bank(u_bank(n))).then_inc(u_raw, 1)

            def res_high(g):
                act.wait_ge(res_ready, g + 1)
                if g >= 2:
                    act.wait_ge(y_mm, 2 * (g - 1))
                nc.scalar.copy(res_hi[:, g % 2, :], resid[g % 2][:, :]).then_inc(res_hi_ready, 1)

            def y_copy(g):
                for half in range(2):
                    act.wait_ge(y_mm, 2 * g + half + 1)
                    nc.scalar.activation(mixT[:, H + g, half * HALF:(half + 1) * HALF], bank(y_bank(g, half)),
                                         ACT.Copy, scale=pscale_c[:, g:g + 1]).then_inc(y_out, 1)

            def qk_high(h, n):
                act.wait_ge(qk_mm, 4 * h + n + 1)
                dst = (q_hi, k_hi)[n % 2]
                nc.scalar.copy(dst[:, (n // 2) * HALF:(n // 2 + 1) * HALF], bank(QK_BANK[n])).then_inc(qk_hi, 1)

            act.wait_ge(xn_ready, NT)
            for n in range(G):
                u_copy(n)
            u_copy(G)
            split_hi(0, 2)
            u_copy(G + 1)
            split_hi(1, 2)
            res_high(0)
            u_copy(G + 2)
            split_hi(2, 2)
            res_high(1)
            u_copy(G + 3)
            act.wait_ge(lam_ready, 1)
            nc.scalar.activation(lam_exp[:, :], lam_sum[:, :], ACT.Exp).then_inc(lam_a, 1)
            qk_high(0, 0)
            y_copy(0)
            res_high(2)
            y_copy(1)

            def v_copy(h, half):
                act.wait_ge(v_mm, 2 * h + half + 1)
                if h:
                    act.wait_ge(t_mm, last_group(h - 1, "V", half))
                elif half == 0:
                    act.wait_ge(res_lo_ready, G)
                nc.scalar.copy(vT[:, half * HALF:(half + 1) * HALF], bank(v_bank(h, half))).then_inc(v_raw, 1)

            def t_high(h, group):
                kind, n, k0, nb = group
                i = t_index(h, group)
                act.wait_ge(t_mm, i + 1)
                if kind == "V":
                    if h:
                        act.wait_ge(pv_mm, NPAIR * h)
                    dst = v_hi[:, k0:k0 + nb, :]
                else:
                    done = NPAIR * h + n // 2
                    if done:
                        act.wait_ge(pv_mm, done)
                    dst = attT_hi[:, k0:k0 + nb, (n % 2) * P:(n % 2 + 1) * P]
                nc.scalar.copy(dst, blocks(4 + i % 2, nb)).then_inc(t_hi, 1)

            def exps(h, s):
                n = NT * h + s
                L = (s + 1) * P
                act.wait_ge(nb_ready, n + 1)
                for r in range(2):
                    nc.scalar.activation(prob[:, s % 2, r, 0:L], prob[:, s % 2, r, 0:L], ACT.Exp,
                                         bias=nbias[:, s % 2, r:r + 1], scale=SCALE,
                                         accum_out=lsum[:, s % 2, r:r + 1]).then_inc(exp_done, 1)

            def o_square(h, j):
                n = NPAIR * h + j
                act.wait_ge(pv_mm, n + 1)
                if n:
                    act.wait_ge(ss_mm, n)
                nc.scalar.activation(o_sq[:, :], PS[:, 6, 0:2 * P], ACT.Square).then_inc(osq_ready, 1)

            def o_rsqrt(h, j):
                n = NPAIR * h + j
                act.wait_ge(ss_mm, n + 1)
                if n:
                    act.wait_ge(mix_ready, n)
                nc.scalar.activation(o_rstd[:, :], PS[:, 6, 2 * P:4 * P], ACT.Ln, bias=eps_c[:, 0:1],
                                     scale=1.0 / VD).then_inc(ln_done, 1)
                act.wait_ge(ln_done, n + 1)
                nc.scalar.activation(o_rstd[:, :], o_rstd[:, :], ACT.Exp, scale=-0.5).then_inc(rstd_ready, 1)

            def wout_high(n):
                e, c = WO_ORDER[n], wo_slot(n)
                count = (1 if c == 3 else 1 + H) + 1 + (n >= 4)
                if n == 0:
                    act.wait_ge(v_mm, 2 * H)
                act.wait_ge(raw_here[c], 16 * count)
                nc.scalar.copy(wout_hi[:, e, :], w_raw[:, c, :]).then_inc(wo_hi, 1)

            def mix_high(t):
                if t == 0:
                    act.wait_ge(qk_mm, 4 * H)
                if t == 2:
                    act.wait_ge(v_mm, 2 * H)
                act.wait_ge(mix_ready, NPAIR * (H - 1) + t // 2 + 1)
                if t >= 4:
                    act.wait_ge(o_mm, 4 * (t // 2 - 1))
                nc.scalar.copy(w_hi[:, t % 4, :].rearrange("p (e n) -> p e n", e=KD),
                               mixT[:, :, t * P:(t + 1) * P]).then_inc(mx_hi, 1)

            act.wait_ge(eps_set, 1)
            for h in range(H):
                if h:
                    for g in t_of_step(h - 1, 8):
                        t_high(h - 1, g)
                    o_square(h - 1, 2)
                qk_high(h, 1)
                if h:
                    for g in t_of_step(h - 1, 9):
                        t_high(h - 1, g)
                    o_rsqrt(h - 1, 2)
                else:
                    res_high(3)
                    y_copy(2)
                for s in range(NT):
                    if h == H - 1 and s == 6:
                        wout_high(0)
                    if h == H - 1 and s == 7:
                        wout_high(2)
                    for g in in_step(h, s):
                        t_high(h, g)
                    if s in (4, 6):
                        o_square(h, (s - 4) // 2)
                    if h == H - 1 and s == 6:
                        v_copy(h, 1)
                        wout_high(1)
                    if s in (5, 7):
                        o_rsqrt(h, (s - 5) // 2)
                    exps(h, s)
                    if s == 0:
                        v_copy(h, 0)
                        if h:
                            o_square(h - 1, 3)
                        else:
                            y_copy(3)
                    if s == 1:
                        qk_high(h, 2)
                        if h:
                            o_rsqrt(h - 1, 3)
                        t_high(h, V0)
                    if s == 2:
                        qk_high(h, 3)
                    if h + 1 < H and s == 3:
                        v_copy(h, 1)
                    if h + 1 < H:
                        if s == 2:
                            act.wait_ge(qk_mm, 4 * h + 3)
                            split_hi(0, 3 + h)
                        if s == 3:
                            act.wait_ge(qk_mm, 4 * h + 4)
                            split_hi(1, 3 + h)
                        if s == 4:
                            act.wait_ge(v_mm, 2 * h + 2)
                            split_hi(2, 3 + h)
                        if s == 7:
                            qk_high(h + 1, 0)
                    else:
                        if s == 5:
                            mix_high(0)
                            mix_high(1)
                        if s == 7:
                            t_high(h, V1)
            h = H - 1
            wout_high(3)
            wout_high(4)
            for g in t_of_step(h, 8):
                t_high(h, g)
            o_square(h, 2)
            for g in t_of_step(h, 9):
                t_high(h, g)
            o_rsqrt(h, 2)
            wout_high(5)
            wout_high(6)
            wout_high(7)
            o_square(h, 3)
            o_rsqrt(h, 3)
            mix_high(2)
            mix_high(3)

            def square_x2(t):
                act.wait_ge(x2_add, 2 * t + 2)
                if t >= 2:
                    act.wait_ge(tr2, 2 * (t - 1))
                nc.scalar.activation(xn2[:, t % 2, :], x2[:, t, :], ACT.Square, accum_out=ss2[:, t:t + 1]).then_inc(sq2, 1)

            def hi_x2(t):
                for j in range(2):
                    act.wait_ge(tr2, 2 * t + j + 1)
                    act.wait_ge(mx_lo, t + 1)
                    nc.scalar.copy(h2T_hi[:, 4 * j:4 * j + 4, t * P:(t + 1) * P],
                                   blocks(tr2_bank(t, j))).then_inc(tr2_hi, 1)

            def gu_high(s, c):
                act.wait_ge(raw_here[c], (s + FIRST_GU[c]) * 16)
                nc.scalar.copy(w_hi[:, c, :], w_raw[:, c, :]).then_inc(fw_hi, 1)

            def dn_high_last():
                act.wait_ge(dn_here, 16 * STEPS)
                act.wait_ge(gu_mm, 8 * (STEPS - 1) + 4)
                nc.scalar.copy(w_hi[:, 0:2, :], dn_raw[:, :, :]).then_inc(fd_hi, 1)

            def dn_high(s):
                act.wait_ge(dn_here, s * 16 + 16)
                nc.scalar.copy(dn_hi[:, :, :], dn_raw[:, :, :]).then_inc(fd_hi, 1)

            FIRST_GU = [1 + H + sum(wo_slot(n) == c for n in range(KD)) + 1 for c in range(3)] \
                + [1 + sum(wo_slot(n) == 3 for n in range(KD)) + 1]

            for p in range(NPAIR):
                square_x2(2 * p)
                square_x2(2 * p + 1)
                if p + 2 < NPAIR:
                    mix_high(2 * p + 4)
                    mix_high(2 * p + 5)
                if p == 2:
                    gu_high(0, 0)
                    gu_high(0, 1)
                if p < NPAIR - 1:
                    hi_x2(2 * p)
                    hi_x2(2 * p + 1)

            def gate_up(s, c, half, slot):
                n = 2 * c + half
                act.wait_ge(gu_mm, s * 8 + 2 * n + 1)
                if not (isinstance(s, int) and s == 0 and n < 2):
                    act.wait_ge(gated_ready, s * 4 + n - 1)
                nc.scalar.activation(silu_g[:, n % 2, :], bank(2 * half), ACT.Silu).then_inc(silu_done, 1)
                act.wait_ge(gated_ready, s * 4 + n + 1)
                nc.scalar.copy(act_hi[:, slot, c, half * HALF:(half + 1) * HALF], gated[:, n % 2, :]).then_inc(act_hi_ready, 1)

            def ff_act(s, slot, first=False, last=False):
                for c in range(2):
                    for half in range(2):
                        if first and c == 0 and half == 0:
                            hi_x2(NT - 2)
                            hi_x2(NT - 1)
                            gu_high(0, 2)
                            gu_high(0, 3)
                        gate_up(s, c, half, slot)
                    if not last:
                        act.wait_ge(gu_mm, s * 8 + (4 * c + 4))
                        gu_high(s + 1, 2 * c)
                        gu_high(s + 1, 2 * c + 1)
                if last:
                    dn_high_last()
                    return
                if not first:
                    act.wait_ge(d_mm, s * 16)
                dn_high(s)

            act.wait_ge(o_mm, 4 * NPAIR)
            ff_act(0, 0, first=True)
            with nc.Fori(0, STEPS // 2 - 1, engines=[ENG.Activation]) as i:
                ff_act(i * 2 + 1, 1)
                ff_act(i * 2 + 2, 0)
            ff_act(STEPS - 2, 1)
            ff_act(STEPS - 1, 0, last=True)

            for t in range(NT):
                for half in range(2):
                    act.wait_ge(d_free, 4 + 16 * (STEPS - 1) + 2 * t + half + 1)
                    n = 2 * t + half
                    if n >= 2:
                        act.wait_ge(sq3, n - 1)
                    nc.scalar.activation(gated[:, n % 2, :], x2[:, t, half * BANK:(half + 1) * BANK], ACT.Square,
                                         accum_out=ss3[:, n:n + 1]).then_inc(sq3, 1)

        @block.vector
        def _(ve):
            chain = [0]

            def link(ins):
                chain[0] += 1
                ins.then_inc(dvec, 1)
                ve.wait_ge(dvec, chain[0])

            def x_norm(t, gains=g1_row[:, :]):
                ve.wait_ge(x_in_here[t], 16)
                ve.wait_ge(pow1, t + 1)
                if t >= 2:
                    ve.wait_ge(tr1, 2 * t - 2)
                nc.vector.scalar_tensor_tensor(out=xn[:, t % 2, :], in0=x_in[:, t, :], scalar=rs1[:, t:t + 1],
                                               in1=gains, op0=ALU.mult, op1=ALU.mult).then_inc(xn_ready, 1)

            def lo_x(t):
                for j in range(2):
                    ve.wait_ge(tr1_hi, 2 * t + j + 1)
                    cols = slice(t * P, (t + 1) * P)
                    nc.vector.tensor_tensor(hT_lo[:, 4 * j:4 * j + 4, cols], blocks(tr1_bank(t, j)),
                                            hT_hi[:, 4 * j:4 * j + 4, cols].bitcast(F32),
                                            ALU.subtract).then_inc(tr1_lo, 1)

            ve.wait_ge(g1_mm, 2)
            g1_psum = PS[:, 0:2, :].rearrange("p b n -> p (b n)")
            x_norm(0, g1_psum)
            x_norm(1, g1_psum)
            lo_x(0)
            lo_x(1)
            x_norm(2, g1_psum)
            nc.vector.tensor_copy(g1_row[:, :], g1_psum).then_inc(g1_set, 1)
            ve.wait_ge(g1_set, 1)
            x_norm(3)
            lo_x(2)
            lo_x(3)
            x_norm(4)
            for t in range(5, NT):
                x_norm(t)
                lo_x(t - 1)
            lo_x(NT - 1)

            ve.wait_ge(small_here, 16 * (2 + G))
            for r in range(2):
                link(nc.vector.tensor_tensor(lam_pr[:, r, :], lam_in[:, 2 * r, :], lam_in[:, 2 * r + 1, :], ALU.mult))
                nc.vector.reduce_sum(lam_sum[:, r:r + 1], lam_pr[:, r, :], mybir.AxisListType.X).then_inc(dvec, 1)
                chain[0] += 1
            ve.wait_ge(dvec, chain[0])
            link(nc.vector.tensor_scalar(subln_c[:, 1:2], subln_c[:, 0:1], 1.0 - LAMBDA_INIT, None, ALU.mult))
            nc.vector.memset(fix[:, :], 0.0).then_inc(lam_ready, 1)

            def pooling(g):
                w = POOL_WINDOWS[g]
                u = mixT[:, H + g, :]
                ve.wait_ge(u_raw, G + g + 1)
                link(nc.vector.tensor_copy(win[0][:, PAD:PAD + 1], u[:, 0:1]))
                link(nc.vector.tensor_tensor(win[0][:, PAD + 1:PAD + SEQ], u[:, 1:SEQ], u[:, 0:SEQ - 1], ALU.add))
                a, reach = 0, 2
                while reach < w:
                    link(nc.vector.tensor_tensor(win[1 - a][:, PAD:PAD + SEQ], win[a][:, PAD:PAD + SEQ],
                                                 win[a][:, PAD - reach:PAD + SEQ - reach], ALU.add))
                    a, reach = 1 - a, 2 * reach
                link(nc.vector.tensor_tensor(fix[:, 0:w - 1], win[a][:, PAD:PAD + w - 1], inv_cnt[:, 0:w - 1], ALU.mult))
                link(nc.vector.tensor_tensor(resid[g % 2][:, 0:w - 1], fix[:, 0:w - 1], u[:, 0:w - 1], ALU.subtract))
                nc.vector.scalar_tensor_tensor(out=resid[g % 2][:, w - 1:SEQ], in0=win[a][:, PAD + w - 1:PAD + SEQ],
                                               scalar=1.0 / w, in1=u[:, w - 1:SEQ], op0=ALU.mult,
                                               op1=ALU.subtract).then_inc(res_ready, 1)
                ve.wait_ge(res_ready, g + 1)

            def res_low(g):
                ve.wait_ge(res_hi_ready, g + 1)
                nc.vector.tensor_tensor(res_lo[:, g % 2, :], resid[g % 2][:, :], res_hi[:, g % 2, :].bitcast(F32),
                                        ALU.subtract).then_inc(res_lo_ready, 1)
                ve.wait_ge(res_lo_ready, g + 1)

            def qk_low(h, n):
                ve.wait_ge(qk_hi, 4 * h + n + 1)
                hi, lo = ((q_hi, q_lo), (k_hi, k_lo))[n % 2]
                cols = slice((n // 2) * HALF, (n // 2 + 1) * HALF)
                nc.vector.tensor_tensor(lo[:, cols], bank(QK_BANK[n]), hi[:, cols].bitcast(F32),
                                        ALU.subtract).then_inc(qk_lo, 1)

            def t_low(h, group):
                kind, n, k0, nb = group
                i = t_index(h, group)
                ve.wait_ge(t_hi, i + 1)
                if kind == "V":
                    lo, hi = v_lo[:, k0:k0 + nb, :], v_hi[:, k0:k0 + nb, :]
                else:
                    cols = slice((n % 2) * P, (n % 2 + 1) * P)
                    lo, hi = attT_lo[:, k0:k0 + nb, cols], attT_hi[:, k0:k0 + nb, cols]
                nc.vector.tensor_tensor(lo, blocks(4 + i % 2, nb), hi.bitcast(F32), ALU.subtract).then_inc(t_lo, 1)

            def mask_max(h, s):
                n = NT * h + s
                L = (s + 1) * P
                ve.wait_ge(s_mm, n + 1)
                if n >= 2:
                    ve.wait_ge(t_mm, last_group(h, "T", s - 2) if s >= 2 else last_group(h - 1, "T", NT + s - 2))
                for r in range(2):
                    nc.vector.tensor_tensor_reduce(
                        out=prob[:, s % 2, r, 0:L],
                        in0=PS[:, 2 * r:2 * r + 2, :].rearrange("p b n -> p (b n)")[:, 0:L],
                        in1=mask[:, SEQ - L:SEQ], scale=1.0, scalar=LOWEST, op0=ALU.add, op1=ALU.max,
                        accum_out=smax[:, s % 2, r:r + 1]).then_inc(s_read, 1)
                ve.wait_ge(s_read, 2 * n + 2)
                nc.vector.tensor_scalar(nbias[:, s % 2, :], smax[:, s % 2, :], -SCALE, None, ALU.mult).then_inc(nb_ready, 1)

            def combine(h, s):
                n = NT * h + s
                L = (s + 1) * P
                ve.wait_ge(exp_done, 2 * n + 2)
                link(nc.vector.reciprocal(rsum[:, s % 2, :], lsum[:, s % 2, :]))
                link(nc.vector.tensor_scalar(prob[:, s % 2, 1, 0:L], prob[:, s % 2, 1, 0:L], rsum[:, s % 2, 1:2],
                                             neg_lam[:, 0:1], ALU.mult, ALU.mult))
                nc.vector.scalar_tensor_tensor(out=prob[:, s % 2, 0, 0:L], in0=prob[:, s % 2, 0, 0:L],
                                               scalar=rsum[:, s % 2, 0:1], in1=prob[:, s % 2, 1, 0:L],
                                               op0=ALU.mult, op1=ALU.add).then_inc(att_ready, 1)

            def o_norm(h, j):
                n = NPAIR * h + j
                ve.wait_ge(rstd_ready, n + 1)
                nc.vector.scalar_tensor_tensor(out=mixT[:, h, j * 2 * P:(j + 1) * 2 * P], in0=PS[:, 6, 0:2 * P],
                                               scalar=subln_c[:, 1:2], in1=o_rstd[:, :], op0=ALU.mult,
                                               op1=ALU.mult).then_inc(mix_ready, 1)

            def mix_low(t):
                ve.wait_ge(mx_hi, t + 1)
                nc.vector.tensor_tensor(w_lo[:, t % 4, :].rearrange("p (e n) -> p e n", e=KD),
                                        mixT[:, :, t * P:(t + 1) * P],
                                        w_hi[:, t % 4, :].bitcast(F32).rearrange("p (e n) -> p e n", e=KD),
                                        ALU.subtract).then_inc(mx_lo, 1)

            ve.wait_ge(pads_set, 2)
            ve.wait_ge(cnt_set, PAD)
            pooling(0)
            pooling(1)
            res_low(0)
            pooling(2)
            res_low(1)
            pooling(3)
            ve.wait_ge(lam_a, 1)
            link(nc.vector.tensor_scalar(neg_lam[:, 1:2], lam_exp[:, 1:2], -LAMBDA_INIT, None, ALU.add))
            link(nc.vector.tensor_tensor(neg_lam[:, 0:1], neg_lam[:, 1:2], lam_exp[:, 0:1], ALU.subtract))
            ve.wait_ge(mask_set, 1)
            qk_low(0, 0)
            res_low(2)
            for h in range(H):
                if h:
                    combine(h - 1, NT - 1)
                    for g in t_of_step(h - 1, 8):
                        t_low(h - 1, g)
                qk_low(h, 1)
                if h:
                    for g in t_of_step(h - 1, 9):
                        t_low(h - 1, g)
                    o_norm(h - 1, 2)
                else:
                    res_low(3)
                for s in range(NT):
                    mask_max(h, s)
                    if s:
                        combine(h, s - 1)
                    if s in (5, 7):
                        o_norm(h, (s - 5) // 2)
                    for g in in_step(h, s):
                        t_low(h, g)
                    if s == 1:
                        qk_low(h, 2)
                        if h:
                            o_norm(h - 1, 3)
                        t_low(h, V0)
                    if s == 2:
                        qk_low(h, 3)
                    if s == NT - 1 and h + 1 < H:
                        qk_low(h + 1, 0)
                    if h == H - 1 and s == 6:
                        mix_low(0)

            h = H - 1
            mix_low(1)
            t_low(h, V1)
            combine(h, NT - 1)
            for g in t_of_step(h, 8) + t_of_step(h, 9):
                t_low(h, g)
            o_norm(h, 2)
            o_norm(h, 3)
            mix_low(2)
            mix_low(3)

            def x2_norm(t):
                ve.wait_ge(pow2, t + 1)
                nc.vector.scalar_tensor_tensor(out=xn2[:, t % 2, :], in0=x2[:, t, :], scalar=rs2[:, t:t + 1],
                                               in1=g2_row[:, :], op0=ALU.mult, op1=ALU.mult).then_inc(xn2_ready, 1)

            def lo_x2(t):
                for j in range(2):
                    ve.wait_ge(tr2_hi, 2 * t + j + 1)
                    cols = slice(t * P, (t + 1) * P)
                    nc.vector.tensor_tensor(h2T_lo[:, 4 * j:4 * j + 4, cols],
                                            blocks(tr2_bank(t, j)),
                                            h2T_hi[:, 4 * j:4 * j + 4, cols].bitcast(F32),
                                            ALU.subtract).then_inc(tr2_lo if t < NT - 2 else d_free, 1)

            ve.wait_ge(g2_here, 16)
            for p in range(NPAIR):
                ve.wait_ge(x2_here[p], 16)
                for i in range(2):
                    for half in range(2):
                        t = 2 * p + i
                        cols = slice(half * BANK, (half + 1) * BANK)
                        ve.wait_ge(o_mm, 2 * t + half + 1)
                        nc.vector.tensor_tensor(x2[:, t, cols], bank(o_bank(t, half)), x2[:, t, cols],
                                                ALU.add).then_inc(x2_add, 1)
                if p + 2 < NPAIR:
                    mix_low(2 * p + 4)
                    mix_low(2 * p + 5)
                x2_norm(2 * p)
                x2_norm(2 * p + 1)
                if p < NPAIR - 1:
                    lo_x2(2 * p)
                    lo_x2(2 * p + 1)

            def gate_up(s, c, half, slot):
                n = 2 * c + half
                ve.wait_ge(gu_mm, s * 8 + (2 * n + 2))
                ve.wait_ge(silu_done, s * 4 + (n + 1))
                nc.vector.tensor_tensor(gated[:, n % 2, :], silu_g[:, n % 2, :], bank(2 * half + 1),
                                        ALU.mult).then_inc(gated_ready, 1)
                ve.wait_ge(act_hi_ready, s * 4 + (n + 1))
                cols = slice(half * HALF, (half + 1) * HALF)
                nc.vector.tensor_tensor(act_lo[:, slot, c, cols], gated[:, n % 2, :],
                                        act_hi[:, slot, c, cols].bitcast(F32), ALU.subtract).then_inc(act_ready, 1)

            def add_down(s, t, half):
                n = 2 * t + half
                cols = slice(half * BANK, (half + 1) * BANK)
                ve.wait_ge(d_mm, s * 16 + (n + 1))
                nc.vector.tensor_tensor(x2[:, t, cols], bank(4 + n % 4), x2[:, t, cols], ALU.add).then_inc(d_free, 1)

            def ff_gate(s, slot, first=False):
                for c in range(2):
                    for half in range(2):
                        if first and c == 0 and half == 0:
                            lo_x2(NT - 2)
                            lo_x2(NT - 1)
                        gate_up(s, c, half, slot)

            def ff_down(s):
                for t in range(NT):
                    for half in range(2):
                        add_down(s, t, half)

            ff_gate(0, 0, first=True)
            with nc.Fori(0, STEPS // 2 - 1, engines=[ENG.DVE]) as i:
                ff_gate(i * 2 + 1, 1)
                ff_down(i * 2)
                ff_gate(i * 2 + 2, 0)
                ff_down(i * 2 + 1)
            ff_gate(STEPS - 2, 1)
            ff_down(STEPS - 3)
            ff_gate(STEPS - 1, 0)
            ff_down(STEPS - 2)

            def y_norm(t):
                ve.wait_ge(pow3, t + 1)
                nc.vector.scalar_tensor_tensor(out=x2[:, t, :], in0=x2[:, t, :], scalar=rs3[:, t:t + 1],
                                               in1=gf_row[:, :], op0=ALU.mult, op1=ALU.mult).then_inc(y_ready, 1)

            ve.wait_ge(gf_here, 16)
            for t in range(NT):
                for half in range(2):
                    add_down(STEPS - 1, t, half)
                if t:
                    y_norm(t - 1)
            for half in range(2):
                cols = slice(half * BANK, (half + 1) * BANK)
                ve.wait_ge(pow3, NT)
                nc.vector.scalar_tensor_tensor(out=x2[:, NT - 1, cols], in0=x2[:, NT - 1, cols],
                                               scalar=rs3[:, NT - 1:NT], in1=gf_row[:, cols], op0=ALU.mult,
                                               op1=ALU.mult).then_inc(y_ready, 1)

        @block.tensor
        def _(pe):
            def three(dst, a_hi, a_lo, b_hi, b_lo, start, stop):
                nc.tensor.matmul(dst, a_hi, b_hi, start=start, stop=False)
                nc.tensor.matmul(dst, a_hi, b_lo, start=False, stop=False)
                return nc.tensor.matmul(dst, a_lo, b_hi, start=False, stop=stop)

            Q_PARTS = {3: (0, 1), 4: (1, 2), 5: (2, 4), 6: (4, 6), 7: (6, 8)}
            V_PARTS = {3: (0, 2), 4: (2, 4), 5: (4, 6), 6: (6, 8)}
            K_SPLIT = 6

            def project(b, c, half, k0=0, k1=KD, part=slice(0, HALF)):
                for k in range(k0, k1):
                    ws = slice(k * P, (k + 1) * P)
                    cols = slice(half * HALF + part.start, half * HALF + part.stop)
                    mm = three(bank(b)[:, part], w_hi[:, c, ws], w_lo[:, c, ws], hT_hi[:, k, cols], hT_lo[:, k, cols],
                               k == 0, k == KD - 1)
                return mm

            def x_tile(t):
                pe.wait_ge(xn_ready, t + 1)
                for j in range(2):
                    if t >= 2:
                        pe.wait_ge(tr1_lo, 2 * t + j - 3)
                    for k in range(4):
                        kk = 4 * j + k
                        tr = nc.tensor.transpose(bank(tr1_bank(t, j))[:, k * P:(k + 1) * P],
                                                 xn[:, t % 2, kk * P:(kk + 1) * P], ident[:, :])
                    tr.then_inc(tr1, 1)

            def u_group(n):
                half, g = divmod(n, G)
                if half == 0:
                    pe.wait_ge(wlo, blk_u(g))
                if n == 2:
                    pe.wait_ge(g1_set, 1)
                if n >= 4:
                    pe.wait_ge(u_raw, n - 3)
                project(u_bank(n), g, half).then_inc(u_mm, 1)

            pe.wait_ge(ones_set, 1)
            pe.wait_ge(g1_here, 16)
            for half in range(2):
                nc.tensor.matmul(bank(half), ones[0:1, :], g1_in[0:1, half * BANK:(half + 1) * BANK],
                                 start=True, stop=True).then_inc(g1_mm, 1)
            pe.wait_ge(ident_set, 1)
            quarters = [slice(0, HALF // 2), slice(HALF // 2, HALF)]
            x_tile(0)
            x_tile(1)
            for g in range(2):
                pe.wait_ge(wlo, blk_u(g))
                pe.wait_ge(tr1_lo, 4)
                project(u_bank(g), g, 0, part=quarters[0])
                if g == 0:
                    x_tile(2)
                    x_tile(3)
            for g in range(2):
                pe.wait_ge(tr1_lo, 8)
                project(u_bank(g), g, 0, part=quarters[1]).then_inc(u_mm, 1)
                x_tile(4 + g)
            u_group(2)
            x_tile(6)
            x_tile(7)
            u_group(3)
            pe.wait_ge(tr1_lo, 2 * NT)
            for n in range(4, 8):
                u_group(n)

            def y_group(g):
                if g == 0:
                    pe.wait_ge(wlo, BLK_PW)
                    pe.wait_ge(u_raw, 2 * G)
                if g >= 2:
                    pe.wait_ge(y_out, 2 * (g - 1))
                pe.wait_ge(res_lo_ready, g + 1)
                for half in range(2):
                    cols = slice(half * HALF, (half + 1) * HALF)
                    three(bank(y_bank(g, half)), pw_hi[:, g, :], pw_lo[:, g, :], res_hi[:, g % 2, cols],
                          res_lo[:, g % 2, cols], True, True).then_inc(y_mm, 1)

            def qk_part(h, n, k0=0, k1=KD):
                if k0 == 0:
                    if n < 2:
                        pe.wait_ge(wlo, blk_qkv(h, n))
                    if n == 0 and h:
                        pe.wait_ge(qk_lo, 4 * h)
                    if n == 1 and h:
                        pe.wait_ge(s_read, 2 * NT * h - 1)
                    if n == 2 and h:
                        pe.wait_ge(s_read, 2 * NT * h)
                    if n == 3:
                        pe.wait_ge(v_raw, 2 * h + 1)
                mm = project(QK_BANK[n], n % 2, n // 2, k0, k1)
                if k1 == KD:
                    mm.then_inc(qk_mm, 1)

            def v_part(h, half, k0=0, k1=KD):
                if half == 0:
                    pe.wait_ge(wlo, blk_qkv(h, 2))
                    pe.wait_ge(qk_lo, 4 * h + 1)
                elif v_bank(h, half) == 7 and k0 == 0:
                    pe.wait_ge(qk_lo, 4 * h + 4)
                elif h == 0:
                    pe.wait_ge(y_out, 2 * G)
                mm = project(v_bank(h, half), 2, half, k0, k1)
                if k1 == KD:
                    mm.then_inc(v_mm, 1)

            def scores(h, s):
                n = NT * h + s
                L = (s + 1) * P
                if n:
                    pe.wait_ge(s_read, 2 * n)
                if s == 0:
                    pe.wait_ge(qk_lo, 4 * h + 2)
                if s == 4:
                    pe.wait_ge(qk_lo, 4 * h + 4)
                    if v_bank(h, 1) == 1:
                        pe.wait_ge(v_raw, 2 * h + 2)
                qs = slice(s * P, (s + 1) * P)
                for k0 in range(0, L, BANK):
                    w = min(BANK, L - k0)
                    ks = slice(k0, k0 + w)
                    for a, b, first, last in ((q_hi, k_hi, True, False), (q_hi, k_lo, False, False),
                                              (q_lo, k_hi, False, True)):
                        for r in range(2):
                            rows = slice(r * HD, (r + 1) * HD)
                            mm = nc.tensor.matmul(PS[:, 2 * r + k0 // BANK, 0:w], a[rows, qs], b[rows, ks],
                                                  start=first, stop=last)
                mm.then_inc(s_mm, 1)

            def transposes(h, group):
                kind, n, k0, nb = group
                i = t_index(h, group)
                if i >= 2:
                    pe.wait_ge(t_lo, i - 1)
                elif i == 0:
                    pe.wait_ge(y_out, 2 * G)
                if kind == "V":
                    pe.wait_ge(v_raw, 2 * h + n + 1)
                else:
                    pe.wait_ge(att_ready, NT * h + n + 1)
                for b in range(nb):
                    kb = k0 + b
                    ks = slice(kb * P, (kb + 1) * P)
                    src = vT[:, ks] if kind == "V" else prob[:, n % 2, 0, ks]
                    tr = nc.tensor.transpose(bank(4 + i % 2)[:, b * P:(b + 1) * P], src, ident[:, :])
                tr.then_inc(t_mm, 1)

            def values(h, j):
                n = NPAIR * h + j
                if n:
                    pe.wait_ge(mix_ready, n)
                pe.wait_ge(t_lo, max(last_group(h, "T", 2 * j + 1), last_group(h, "V", 1 if j >= 2 else 0)))
                for kb in range(2 * j + 2):
                    c0 = 0 if kb <= 2 * j else P
                    mm = three(PS[:, 6, c0:2 * P], v_hi[:, kb, :], v_lo[:, kb, :], attT_hi[:, kb, c0:2 * P],
                               attT_lo[:, kb, c0:2 * P], kb == 0, kb == 2 * j + 1)
                mm.then_inc(pv_mm, 1)

            def square_sum(h, j):
                n = NPAIR * h + j
                pe.wait_ge(osq_ready, n + 1)
                nc.tensor.matmul(PS[:, 6, 2 * P:4 * P], ones[:, :], o_sq[:, :], start=True, stop=True).then_inc(ss_mm, 1)

            pe.wait_ge(ones_set, 1)
            qk_part(0, 0)
            y_group(0)
            y_group(1)
            for h in range(H):
                if h:
                    qk_part(h, 1, 0, K_SPLIT)
                    for g in t_of_step(h - 1, 8):
                        transposes(h - 1, g)
                    values(h - 1, 2)
                    qk_part(h, 1, K_SPLIT, KD)
                    for g in t_of_step(h - 1, 9):
                        transposes(h - 1, g)
                    square_sum(h - 1, 2)
                else:
                    qk_part(h, 1)
                    y_group(2)
                for s in range(NT):
                    scores(h, s)
                    for g in in_step(h, s):
                        transposes(h, g)
                    if s == 0:
                        v_part(h, 0)
                        if h:
                            values(h - 1, 3)
                        else:
                            y_group(3)
                    if s == 1:
                        qk_part(h, 2)
                        if h:
                            square_sum(h - 1, 3)
                        transposes(h, V0)
                    if s == 2:
                        qk_part(h, 3)
                    if s in (4, 6):
                        values(h, (s - 4) // 2)
                    if h + 1 < H:
                        if s == 3:
                            v_part(h, 1)
                        if s in Q_PARTS:
                            qk_part(h + 1, 0, *Q_PARTS[s])
                    elif s in V_PARTS:
                        v_part(h, 1, *V_PARTS[s])
                    if s in (5, 7):
                        square_sum(h, (s - 5) // 2)
            def out_project(t, n):
                e = WO_ORDER[n]
                if t < 2:
                    pe.wait_ge(wo_lo, n + 1)
                es = slice(e * P, (e + 1) * P)
                for half in range(2):
                    if t == n == 0 and half == 1:
                        pe.wait_ge(s_read, 2 * NT * H - 1)
                    cols = slice(half * BANK, (half + 1) * BANK)
                    mm = three(bank(o_bank(t, half)), w_hi[:, t % 4, es], w_lo[:, t % 4, es],
                               wout_hi[:, e, cols], wout_lo[:, e, cols], n == 0, n == KD - 1)
                    if n == KD - 1:
                        mm.then_inc(o_mm, 1)

            def x2_tiles(p):
                if p == NPAIR - 1:
                    pe.wait_ge(x2_add, 2 * NT)
                for t in (2 * p, 2 * p + 1):
                    pe.wait_ge(xn2_ready, t + 1)
                    for j in range(2):
                        b = tr2_bank(t, j)
                        for k in range(4):
                            kk = 4 * j + k
                            tr = nc.tensor.transpose(bank(b)[:, k * P:(k + 1) * P], xn2[:, t % 2, kk * P:(kk + 1) * P],
                                                     ident[:, :])
                        tr.then_inc(tr2, 1)

            h = H - 1
            pe.wait_ge(v_raw, 2 * H)
            pe.wait_ge(mx_lo, 1)
            out_project(0, 0)
            out_project(0, 1)
            out_project(0, 2)
            transposes(h, V1)
            first, second = t_of_step(h, 8)
            transposes(h, first)
            pe.wait_ge(s_read, 2 * NT * H)
            pe.wait_ge(mx_lo, 2)
            out_project(1, 0)
            transposes(h, second)
            values(h, 2)
            out_project(1, 1)
            for g in t_of_step(h, 9):
                transposes(h, g)
            square_sum(h, 2)
            out_project(1, 2)
            for i in range(2):
                out_project(i, 3)
            values(h, 3)
            for n in (4, 5):
                out_project(0, n)
                out_project(1, n)
            square_sum(h, 3)
            for n in (6, 7):
                out_project(0, n)
                out_project(1, n)
            for p in range(1, NPAIR):
                pe.wait_ge(mx_lo, 2 * p + 2)
                if p == 1:
                    pe.wait_ge(t_lo, len(T_SEQ))
                    pe.wait_ge(mix_ready, H * NPAIR)
                else:
                    pe.wait_ge(tr2_lo, 4 * (p - 1))
                for n in range(KD):
                    if n == KD // 2:
                        x2_tiles(p - 1)
                    out_project(2 * p, n)
                    out_project(2 * p + 1, n)

            def gate_up(s, c, half, kinds=range(2)):
                n = 2 * c + half
                if not (isinstance(s, int) and s == 0 and n < 2):
                    pe.wait_ge(gated_ready, s * 4 + (n - 1))
                for kind in kinds:
                    slot = 2 * c + kind
                    if half == 0:
                        pe.wait_ge(fw_lo, s * 4 + (slot + 1))
                    cols = slice(half * HALF, (half + 1) * HALF)
                    for k in range(KD):
                        ws = slice(k * P, (k + 1) * P)
                        mm = three(bank(2 * half + kind), w_hi[:, slot, ws], w_lo[:, slot, ws],
                                   h2T_hi[:, k, cols], h2T_lo[:, k, cols], k == 0, k == KD - 1)
                    mm.then_inc(gu_mm, 1)

            def ff_gate(s):
                for c in range(2):
                    for half in range(2):
                        gate_up(s, c, half)

            def ff_down(s, slot, hi=dn_hi, lo=dn_lo):
                pe.wait_ge(act_ready, s * 4 + 4)
                pe.wait_ge(fd_lo, s + 1)
                for t in range(NT):
                    ts = slice(t * P, (t + 1) * P)
                    for half in range(2):
                        n = 2 * t + half
                        pe.wait_ge(d_free, s * 16 + (n + 1))
                        cols = slice(half * BANK, (half + 1) * BANK)
                        for c in range(2):
                            mm = three(bank(4 + n % 4), act_hi[:, slot, c, ts], act_lo[:, slot, c, ts],
                                       hi[:, c, cols], lo[:, c, cols], c == 0, c == 1)
                        mm.then_inc(d_mm, 1)

            pe.wait_ge(tr2_lo, 4 * (NPAIR - 1))
            gate_up(0, 0, 0, (0,))
            x2_tiles(NPAIR - 1)
            gate_up(0, 0, 0, (1,))
            pe.wait_ge(d_free, 4)
            gate_up(0, 0, 1)
            gate_up(0, 1, 0)
            gate_up(0, 1, 1)
            with nc.Fori(0, STEPS // 2 - 1, engines=[ENG.PE]) as i:
                ff_gate(i * 2 + 1)
                ff_down(i * 2, 0)
                ff_gate(i * 2 + 2)
                ff_down(i * 2 + 1, 1)
            ff_gate(STEPS - 2)
            ff_down(STEPS - 3, 0)
            ff_gate(STEPS - 1)
            ff_down(STEPS - 2, 1)
            ff_down(STEPS - 1, 0, w_hi, w_lo)


_INS = ["x", "norm1_g", "w_in", "lam_qk", "subln_g", "pool_w", "pool_scale", "w_out",
        "norm2_g", "w_gate", "w_up", "w_down", "final_g"]


def kernel(**inputs):
    import numpy as _np
    import concourse.bacc as _bacc
    from concourse import mybir as _mybir
    from concourse.bass_utils import run_bass_kernel_spmd as _run

    nc = _bacc.Bacc("TRN2", target_bir_lowering=False, num_devices=1, dynamic_dma_scratch_size=DMA_SCRATCH)
    arrays, args = {}, []
    for name in _INS:
        a = _np.ascontiguousarray(inputs[name])
        arrays[f"in_{name}_dram"] = a
        args.append(nc.dram_tensor(f"in_{name}_dram", a.shape, _mybir.dt.from_np(a.dtype), kind="ExternalInput").ap())
    shape = _np.shape(inputs["x"])
    args.append(nc.dram_tensor("out_0_dram", shape, _mybir.dt.float32, kind="ExternalOutput").ap())
    hybrid_block(nc, *args)
    r = _run(nc, [arrays], core_ids=[0])
    return r.results[0]["out_0_dram"]
```
